# Optimizing a Trainium2 kernel written in Bass

```python
import jax
import jax.numpy as jnp
from jax import lax
import numpy as np

D_MODEL = 1024
BATCH = 1
SEQ = 512
DEPTH = 2

N_A_LAYERS = DEPTH // 2
N_B_LAYERS = DEPTH - N_A_LAYERS
EPS = 1e-6

GLA_HEADS = 4
GLA_DK = D_MODEL // 2
GLA_DV = D_MODEL
GLA_HK = GLA_DK // GLA_HEADS
GLA_HV = GLA_DV // GLA_HEADS
GLA_GATE_RANK = 16
GLA_GATE_NORM = 16.0
GLA_CHUNK = 64
GLA_IN = 2 * GLA_DK + 2 * GLA_DV + GLA_GATE_RANK

FOX_HD = 64
FOX_HEADS = D_MODEL // FOX_HD
FOX_QBLOCK = 128
FOX_FGATE_BIAS = 2.0

PEER_HEADS = 8
PEER_NKEYS = 128
PEER_EXPERTS = PEER_NKEYS * PEER_NKEYS
PEER_TOPK = 16
PEER_DQ = 256
PEER_TOKBLOCK = 128

kernel_name = "yoco_gla_fox_peer_adaln"

F32 = jnp.float32

def _rms(x):
    x32 = x.astype(F32)
    return x32 * lax.rsqrt(jnp.mean(x32 * x32, axis=-1, keepdims=True) + EPS)

def rmsnorm_gain(x, g):
    return (_rms(x) * g.astype(F32)).astype(x.dtype)

def adaln(x, shift, scale):
    y = _rms(x) * (1.0 + scale[:, None, :].astype(F32)) + shift[:, None, :].astype(F32)
    return y.astype(x.dtype)

def gla_mixer(h, w_in, w_gate2, b_gate, o_norm, w_out):
    B, S, _ = h.shape
    C, H = GLA_CHUNK, GLA_HEADS
    nc = S // C
    proj = h @ w_in
    q, k, v, g, glow = jnp.split(
        proj, [GLA_DK, 2 * GLA_DK, 2 * GLA_DK + GLA_DV, 2 * GLA_DK + 2 * GLA_DV], axis=-1)
    gk = jax.nn.log_sigmoid((glow @ w_gate2 + b_gate).astype(F32)) / GLA_GATE_NORM

    def heads(t, hd):
        return t.reshape(B, nc, C, H, hd).transpose(1, 0, 3, 2, 4)

    qc = heads(q * (GLA_HK ** -0.5), GLA_HK)
    kc = heads(k, GLA_HK)
    vc = heads(v, GLA_HV)
    gc = heads(gk, GLA_HK)
    causal = jnp.tril(jnp.ones((C, C), dtype=bool))

    def step(state, inp):
        qb, kb, vb, gb = inp
        b = jnp.cumsum(gb, axis=-2)
        qf = qb.astype(F32)
        kf = kb.astype(F32)
        vf = vb.astype(F32)
        o_inter = jnp.einsum('bhtk,bhkv->bhtv', qf * jnp.exp(b), state)
        rel = jnp.where(causal[:, :, None], b[..., :, None, :] - b[..., None, :, :], -jnp.inf)
        attn = jnp.einsum('bhtk,bhsk,bhtsk->bhts', qf, kf, jnp.exp(rel))
        o = o_inter + jnp.einsum('bhts,bhsv->bhtv', attn, vf)
        b_last = b[..., -1:, :]
        state = (jnp.exp(b[..., -1, :])[..., None] * state
                 + jnp.einsum('bhsk,bhsv->bhkv', kf * jnp.exp(b_last - b), vf))
        return state, o.astype(vb.dtype)

    state0 = jnp.zeros((B, H, GLA_HK, GLA_HV), F32)
    _, o = lax.scan(step, state0, (qc, kc, vc, gc))
    o = o.transpose(1, 0, 3, 2, 4).reshape(B, S, H, GLA_HV)
    o = rmsnorm_gain(o, o_norm) * jax.nn.silu(g.reshape(B, S, H, GLA_HV))
    return o.reshape(B, S, GLA_DV) @ w_out

def fox_shared_kv(hk, w_kvf, b_f, k_norm):
    B, S, _ = hk.shape
    proj = hk @ w_kvf
    k, v, f = jnp.split(proj, [D_MODEL, 2 * D_MODEL], axis=-1)
    k = rmsnorm_gain(k.reshape(B, S, FOX_HEADS, FOX_HD), k_norm).transpose(0, 2, 1, 3)
    v = v.reshape(B, S, FOX_HEADS, FOX_HD).transpose(0, 2, 1, 3)
    log_f = jax.nn.log_sigmoid(f.astype(F32) + b_f.astype(F32))
    cum = jnp.cumsum(log_f, axis=1).transpose(0, 2, 1)
    return k, v, cum

def fox_mixer(h, k, v, cum, w_qg, q_norm, w_out):
    B, S, _ = h.shape
    QB = FOX_QBLOCK
    q, g = jnp.split(h @ w_qg, [D_MODEL], axis=-1)
    q = rmsnorm_gain(q.reshape(B, S, FOX_HEADS, FOX_HD), q_norm).transpose(0, 2, 1, 3)
    scale = FOX_HD ** -0.5
    diag = jnp.tril(jnp.ones((QB, QB), dtype=bool))
    outs = []
    for i in range(S // QB):
        lo, hi = i * QB, (i + 1) * QB
        s = jnp.einsum('bhqd,bhkd->bhqk', q[:, :, lo:hi], k[:, :, :hi]).astype(F32) * scale
        s = s + cum[:, :, lo:hi, None] - cum[:, :, None, :hi]
        mask = jnp.concatenate([jnp.ones((QB, lo), dtype=bool), diag], axis=1)
        p = jax.nn.softmax(jnp.where(mask, s, -jnp.inf), axis=-1)
        outs.append(jnp.einsum('bhqk,bhkd->bhqd', p.astype(v.dtype), v[:, :, :hi]))
    o = jnp.concatenate(outs, axis=2).transpose(0, 2, 1, 3).reshape(B, S, D_MODEL)
    o = o * jax.nn.sigmoid(g)
    return o @ w_out

def peer_ffn(h, w_q, sub_keys, u_tab, v_tab):
    B, S, D = h.shape
    TB, K, NK, PH = PEER_TOKBLOCK, PEER_TOPK, PEER_NKEYS, PEER_HEADS
    xt = h.reshape((B * S) // TB, TB, D)

    def block(xb):
        q = (xb @ w_q).reshape(TB, PH, 2, PEER_DQ // 2)
        s = jnp.einsum('thpd,hpnd->thpn', q, sub_keys).astype(F32)
        s_half, i_half = lax.top_k(s, K)
        cand = (s_half[:, :, 0, :, None] + s_half[:, :, 1, None, :]).reshape(TB, PH, K * K)
        top_s, top_c = lax.top_k(cand, K)
        i0 = jnp.take_along_axis(i_half[:, :, 0], top_c // K, axis=-1)
        i1 = jnp.take_along_axis(i_half[:, :, 1], top_c % K, axis=-1)
        idx = i0 * NK + i1
        gate = jax.nn.softmax(top_s, axis=-1)
        a = jax.nn.gelu(jnp.einsum('td,thkd->thk', xb, u_tab[idx]).astype(F32), approximate=False)
        w = (gate * a).astype(xb.dtype)
        return jnp.einsum('thk,thkd->td', w, v_tab[idx])

    return lax.map(block, xt).reshape(B, S, D)

def setup_inputs(seed: int = 0) -> dict:
    key = jax.random.key(seed)
    ks = jax.random.split(key, 21)

    def nrm(k, shape, scale):
        return jax.random.normal(k, shape, F32) * scale

    NA, NB, D = N_A_LAYERS, N_B_LAYERS, D_MODEL
    return {
        'x': nrm(ks[0], (BATCH, SEQ, D), 1.0),
        'c': nrm(ks[1], (BATCH, D), 1.0),
        'mod_w': nrm(ks[2], (DEPTH, D, 6 * D), 0.5 * D ** -0.5),
        'mod_b': nrm(ks[3], (DEPTH, 6 * D), 0.02),
        'gla_w_in': nrm(ks[4], (NA, D, GLA_IN), D ** -0.5),
        'gla_w_gate2': nrm(ks[5], (NA, GLA_GATE_RANK, GLA_DK), GLA_GATE_RANK ** -0.5),
        'gla_b_gate': nrm(ks[6], (NA, GLA_DK), 0.02),
        'gla_o_norm': 1.0 + nrm(ks[7], (NA, GLA_HV), 0.02),
        'gla_w_out': nrm(ks[8], (NA, GLA_DV, D), GLA_DV ** -0.5),
        'kv_mod_w': nrm(ks[9], (D, 2 * D), 0.5 * D ** -0.5),
        'kv_mod_b': nrm(ks[10], (2 * D,), 0.02),
        'fox_w_kvf': nrm(ks[11], (D, 2 * D + FOX_HEADS), D ** -0.5),
        'fox_b_f': FOX_FGATE_BIAS + nrm(ks[12], (FOX_HEADS,), 0.1),
        'fox_k_norm': 1.0 + nrm(ks[13], (FOX_HD,), 0.02),
        'fox_w_qg': nrm(ks[14], (NB, D, 2 * D), D ** -0.5),
        'fox_q_norm': 1.0 + nrm(ks[15], (NB, FOX_HD), 0.02),
        'fox_w_out': nrm(ks[16], (NB, D, D), D ** -0.5),
        'peer_w_q': nrm(ks[17], (DEPTH, D, PEER_HEADS * PEER_DQ), D ** -0.5),
        'peer_sub_keys': nrm(ks[18], (DEPTH, PEER_HEADS, 2, PEER_NKEYS, PEER_DQ // 2), (PEER_DQ // 2) ** -0.5),
        'peer_u': nrm(ks[19], (DEPTH, PEER_EXPERTS, D), D ** -0.5),
        'peer_v': nrm(ks[20], (DEPTH, PEER_EXPERTS, D), PEER_HEADS ** -0.5),
    }

def reference(x, c, mod_w, mod_b, gla_w_in, gla_w_gate2, gla_b_gate, gla_o_norm, gla_w_out,
              kv_mod_w, kv_mod_b, fox_w_kvf, fox_b_f, fox_k_norm, fox_w_qg, fox_q_norm, fox_w_out,
              peer_w_q, peer_sub_keys, peer_u, peer_v):
    shared = None
    for layer in range(DEPTH):
        if layer == N_A_LAYERS:
            kv_shift, kv_scale = jnp.split(c @ kv_mod_w + kv_mod_b, 2, axis=-1)
            shared = fox_shared_kv(adaln(x, kv_shift, kv_scale), fox_w_kvf, fox_b_f, fox_k_norm)
        mod = c @ mod_w[layer] + mod_b[layer]
        sh1, sc1, g1, sh2, sc2, g2 = jnp.split(mod, 6, axis=-1)
        h = adaln(x, sh1, sc1)
        if layer < N_A_LAYERS:
            mix = gla_mixer(h, gla_w_in[layer], gla_w_gate2[layer], gla_b_gate[layer],
                            gla_o_norm[layer], gla_w_out[layer])
        else:
            j = layer - N_A_LAYERS
            k_sh, v_sh, cum_sh = shared
            mix = fox_mixer(h, k_sh, v_sh, cum_sh, fox_w_qg[j], fox_q_norm[j], fox_w_out[j])
        x = x + g1[:, None, :] * mix
        h = adaln(x, sh2, sc2)
        x = x + g2[:, None, :] * peer_ffn(h, peer_w_q[layer], peer_sub_keys[layer],
                                          peer_u[layer], peer_v[layer])
    return x


_drawn_inputs = setup_inputs


def setup_inputs(seed=0):
    import zlib

    import numpy as np

    out = dict(_drawn_inputs(seed))
    spreads = {}
    factors = {'gla_b_gate': 4.718,
     'gla_o_norm': 3.425,
     'kv_mod_b': 5.52,
     'fox_b_f': 49.448,
     'fox_k_norm': 8.0,
     'fox_q_norm': 8.0}
    for name, (base, spread) in spreads.items():
        noise = np.random.default_rng([zlib.crc32(name.encode()), seed]).standard_normal(out[name].shape)
        drawn = base * np.exp(spread * noise) if base else spread * noise
        out[name] = jnp.asarray(drawn.astype(out[name].dtype))
    for name, factor in factors.items():
        out[name] = (out[name] * factor).astype(out[name].dtype)
    return out
```

```python
from contextlib import ExitStack

import concourse.bass as bass
from concourse import mybir

F32 = mybir.dt.float32
U32 = mybir.dt.uint32
U8 = mybir.dt.uint8
ALU = mybir.AluOpType
ACT = mybir.ActivationFunctionType
AX_X = mybir.AxisListType.X

P = 128
D = 1024
SEQ = 512
DC = D // P
HALF = 256
NHALF = SEQ // HALF
TBH = HALF // P
EPS = 1e-6
GLA_H, GLA_HK, GLA_HV, RANK = 4, 128, 256, 16
FOX_H, FOX_HD = 16, 64
PH, NK, TOPK = 8, 128, 16
EXPERTS = NK * NK
HP = 2 * PH
NSEL = PH * TOPK
LEVELS = [64, 32, 16, 8, 4, 2, 1]
NEG = -3.0e38

TILES = {}
_n = 0
for _name, _count in (("mod0", 48), ("mod1", 48), ("kvmod", 16), ("gla_in", 24), ("gla_out", 8),
                      ("pq0", 16), ("pq1", 16), ("keys0", 2), ("keys1", 2), ("fox_kv", 16),
                      ("fox_qg", 16), ("fox_out", 8)):
    TILES[_name] = _n
    _n += _count
NTILES = _n
WR = 4

COL_C = 0
COL_MODB = COL_C + DC
NMOD = 112
COL_BG = COL_MODB + NMOD
COL_ON = COL_BG + GLA_H
COL_KN = COL_ON + 2
COL_QN = COL_KN + 1
COL_BF = COL_QN + 1
NCOL = COL_BF + 1
K_ID, K_ONE, K_BD, K_NEG, K_ZERO, K_IOTA = 0, 128, 256, 384, 512, 640
NCONST = K_IOTA + 16

NSLOT = 8
PAIR = 2

SEMS = """x_loaded mask_loaded mixed const_loaded col_loaded small_loaded tile_started mod_tiles mods_ready
 sq_ready ms_ready rms_ready xn_ready h_ready hk_ready glow_ready gate_abs gate_soft qk_ready
 g_ready v_ready level_gap level_exp ql_ready kl_ready attn_ready last_gap last_exp chunk_exp
 kd_ready ot_ready state_ready sqo_ready mso_ready rmso_ready silu_exp o_ready
 htok_ready qp_ready s_ready s_free top_ready top_exp route_ready
 slots_used dot_ready gelu_ready diag_ready idx_staged acc_full otok_ready acc_free dots_done
 fgate_abs fgate_soft cum_ready fk_raw fq_raw fg_raw fv_ready fsq_ready fms_ready frms_ready fn_ready
 negmax_ready p_ready pn_ready pt_ready fo_ready fsig_exp fgated
 act_chain dve_chain out_written""".split()


def build(nc, xt, wt, uv, cols, consts, masks, small, wgate, out):
    ctx = ExitStack()
    with ctx:
        def sb(name, shape, dt=F32):
            return ctx.enter_context(nc.sbuf_tensor(name, shape, dt))

        xT = sb("xT", [P, DC, SEQ])
        hT = sb("hT", [P, DC, HALF])
        wring = sb("wring", [P, WR, DC, P])
        const = sb("const", [P, NCONST])
        col = sb("col", [P, NCOL])
        levmask = sb("levmask", [P, 8, P], U8)
        wsmall = sb("wsmall", [P, 2, DC, 16])
        wg2 = sb("wg2", [RANK, GLA_H * GLA_HK])
        mod = sb("mod", [P, NMOD])
        mod1 = sb("mod1", [P, NMOD])
        rms = sb("rms", [P, HALF])
        qn8 = sb("qn8", [P, 1])
        ring = sb("ring", [P, NSLOT, 2 * D])
        diag = sb("diag", [P, NSLOT, P])
        dots = sb("dots", [P, NSLOT])
        acts = sb("acts", [P, NSLOT])
        idx_now = sb("idx_now", [P, NSLOT], U32)
        htok = sb("htok", [P, 2, TBH, D])
        idx = sb("idx", [P, 2, TBH * NSEL], U32)
        gate = sb("gate", [P, 2, TBH * NSEL])
        ncum = sb("ncum", [FOX_H, SEQ])
        kvmem = sb("kvmem", [P, 8192])
        tmp = sb("tmp", [P, 9216])

        def view(mem, at, *dims, dt=None):
            n = 1
            for d in dims:
                n *= d
            v = mem[:, at:at + n]
            if dt is not None:
                v = v.bitcast(dt)
            names = "abc"[:len(dims)]
            if len(dims) == 1:
                return v
            return v.rearrange(f"p ({' '.join(names)}) -> p {' '.join(names)}",
                               **{k: d for k, d in zip(names[1:], dims[1:])})

        g_q = view(tmp, 0, GLA_H, HALF)
        g_k = view(tmp, 1024, GLA_H, HALF)
        g_b = view(tmp, 2048, GLA_H * HALF)
        g_d = view(tmp, 3072, GLA_H * HALF)
        g_e = view(tmp, 4096, GLA_H * HALF)
        g_ql = view(tmp, 5120, GLA_H, HALF)
        g_kl = view(tmp, 6144, GLA_H, HALF)
        g_attn = view(tmp, 7168, TBH, GLA_H, P)
        g_kd = view(tmp, 8192, TBH, GLA_H, P)
        g_sq = view(tmp, 3072, DC, HALF)
        g_rs = view(tmp, 5120, GLA_H, HALF)
        g_low = kvmem[0:RANK, 7168:7168 + HALF]
        g_el = view(kvmem, 7168 + HALF, GLA_H * TBH)
        g_g = view(kvmem, 0, DC, HALF)
        g_v = view(kvmem, 2048, TBH, D)
        g_o = view(kvmem, 4096, DC, HALF)
        g_state = view(kvmem, 6144, GLA_H, GLA_HV)
        r_q = view(tmp, 0, HP, HALF)
        r_s = view(tmp, 4096, HP, NK)
        r_hot = view(tmp, 4096, NSEL, TOPK)
        r_cand = view(tmp, 6144, PH, TOPK * TOPK)
        r_v = view(tmp, 8192, HP, TOPK)
        r_i = view(tmp, 8448, HP, TOPK, dt=U32)
        r_if = view(tmp, 8704, HP, TOPK)
        r_ts = view(tmp, 8960, PH, TOPK)
        r_tc = view(tmp, 9088, PH, TOPK, dt=U32)
        r_hu = view(tmp, 6144, NSEL, dt=U32)
        r_hf = view(tmp, 6272, NSEL)
        r_sel = view(tmp, 6400, 2, NSEL)
        r_sum = view(tmp, 6656, PH)
        r_max = view(tmp, 6664, PH)
        f_hk = view(tmp, 0, DC, HALF)
        f_o = f_hk
        f_q = view(tmp, 2048, DC, HALF)
        f_g = view(tmp, 4096, DC, HALF)
        f_p = view(tmp, 6144, 2, SEQ)
        f_pt = view(tmp, 7168, 2, SEQ)
        f_e = view(tmp, 6144, DC, HALF)
        f_sq = view(tmp, 6144, 4, HALF)
        f_rs = view(tmp, 7168, 4, HALF)
        f_z = tmp[0:FOX_H, 8192:8192 + HALF]
        f_a = tmp[0:FOX_H, 8448:8448 + HALF]
        f_k = view(kvmem, 0, DC, SEQ)
        f_v = view(kvmem, 4096, SEQ // P, D)
        f_nm = sb("f_nm", [P, 2])
        f_sum = sb("f_sum", [P, 2])
        f_inv = sb("f_inv", [P, 2])

        acc = ctx.enter_context(nc.psum_tensor("acc", [P, 2, 512], F32))
        banks = [ctx.enter_context(nc.psum_tensor(f"bank{i}", [P, 512], F32)) for i in range(6)]

        sem = {n: ctx.enter_context(nc.semaphore(n)) for n in SEMS}
        w_ready = [ctx.enter_context(nc.semaphore(f"w_ready{i}")) for i in range(WR)]
        row_ready = [ctx.enter_context(nc.semaphore(f"row_ready{i}")) for i in range(NSLOT)]
        x_mix = [[ctx.enter_context(nc.semaphore(f"x_mix{l}{h}")) for h in range(2)] for l in range(2)]
        x_ffn = [[ctx.enter_context(nc.semaphore(f"x_ffn{l}{h}")) for h in range(2)] for l in range(2)]
        bank_full = [ctx.enter_context(nc.semaphore(f"bank_full{i}")) for i in range(6)]
        bank_taken = [ctx.enter_context(nc.semaphore(f"bank_taken{i}")) for i in range(6)]

        ident, ones, blockdiag = const[:, K_ID:K_ID + P], const[:, K_ONE:K_ONE + P], const[:, K_BD:K_BD + P]
        negmask = const[:, K_NEG:K_NEG + P]
        zeros = const[:, K_ZERO:K_ZERO + P]
        iota = const[:, K_IOTA:K_IOTA + TOPK]

        PLAN = [(None, [("gla", 0, 0), ("route", 0, 0)]),
                (0, [("gla", 0, 1), ("route", 0, 1)]),
                (1, [("fox", 1, 0), ("route", 1, 0)]),
                (2, [("fox", 1, 1), ("route", 1, 1)]),
                (3, [])]
        ORDER = [key for _, stages in PLAN for key in stages]
        LN = {s: n for n, s in enumerate(ORDER)}
        RT = {s[1:]: n for n, s in enumerate([s for s in ORDER if s[0] == "route"])}
        GATHER = {n: key for key, n in RT.items()}

        fills = {}
        nfill, nfull = [0] * 6, [0] * 6
        order_of_tiles = []

        BLOCK_STEPS = NSEL // PAIR
        HALF_STEPS = TBH * BLOCK_STEPS
        position = {}
        window = [0, 0]

        def full(eng, name):
            keep_up[eng.engine](position[name])
            b, _, n = fills[name]
            eng.wait_ge(bank_full[b], n)

        def taken(eng, name):
            keep_up[eng.engine](position[name])
            b, n, _ = fills[name]
            eng.wait_ge(bank_taken[b], n)

        keep_up = {}

        def bank_of(name):
            return banks[fills[name][0]]

        def freed(ins, name):
            ins.then_inc(bank_taken[fills[name][0]], 1)

        def open_window(q):
            window[1] = 0 if q is None else (q + 1) * HALF_STEPS

        block = ctx.enter_context(nc.Block())

        @block.tensor
        def _(pe):
            keep_up[pe.engine] = lambda x: None
            open_window(None)
            begun = [0]
            credit = [0.0]

            def step(s):
                b = s // BLOCK_STEPS
                if s % BLOCK_STEPS == 0:
                    open_sums(b)
                for k in range(PAIR * s, PAIR * s + PAIR):
                    r = k % NSLOT
                    pe.wait_ge(sem["diag_ready"], k + 1)
                    sum_rows(r)
                begun[0] = s + 1
                if (s + 1) % BLOCK_STEPS == 0:
                    close_sums(b)

            def open_sums(b):
                if b:
                    pe.wait_ge(sem["acc_free"], b)
                for c in range(2):
                    mm = pe.matmul(acc[:, c], zeros, const[:, 0:512], start=True, stop=False)
                if b == 0:
                    mm.then_inc(sem["slots_used"], NSLOT)

            def sum_rows(r):
                for c in range(2):
                    mm = pe.matmul(acc[:, c], diag[:, r], ring[:, r, D + 512 * c:D + 512 * (c + 1)],
                                   start=False, stop=False)
                mm.then_inc(sem["slots_used"], 1)

            def close_sums(b):
                for c in range(2):
                    mm = pe.matmul(acc[:, c], zeros, const[:, 0:512], start=False, stop=True)
                mm.then_inc(sem["acc_full"], 1)
                pe.wait_ge(sem["otok_ready"], b + 1)
                for c in range(DC):
                    mm = pe.transpose(acc[:, c // 4, (c % 4) * P:(c % 4 + 1) * P],
                                      htok[:, b // TBH % 2, b % TBH, c * P:(c + 1) * P], ident)
                mm.then_inc(sem["acc_full"], 1)

            def weave(us, quota=None):
                credit[0] += us
                while credit[0] >= pace[0]:
                    credit[0] -= pace[0]
                    if begun[0] < window[1]:
                        step(begun[0])

            def fill_gap(steps):
                for _ in range(steps):
                    if begun[0] < window[1]:
                        step(begun[0])

            pace = [3.0]

            def bank(name, b):
                if nfill[b]:
                    pe.wait_ge(bank_taken[b], nfill[b])
                nfill[b] += 1
                fills[name] = (b, nfill[b], None)
                position[name] = begun[0]
                return banks[b]

            def done(mm, name):
                b, n, _ = fills[name]
                nfull[b] += 1
                fills[name] = (b, n, nfull[b])
                position[name] = begun[0]
                mm.then_inc(bank_full[b], 1)

            def tile(which):
                j = len(order_of_tiles)
                order_of_tiles.append(which)
                pe.wait_ge(w_ready[j % WR], 16 * (j // WR + 1))
                return wring[:, j % WR], j

            def project(which, name, src, token_major=False):
                weave(3.5)
                w, j = tile(which)
                b = bank(name, 4 + j % 2)
                if not token_major:
                    for c in range(DC):
                        mm = pe.matmul(b[:, 0:HALF], w[:, c], src[:, c], start=c == 0, stop=c == DC - 1)
                        if c == 0:
                            mm.then_inc(sem["tile_started"], 1)
                else:
                    for tb in range(TBH):
                        for c in range(DC):
                            mm = pe.matmul(b[:, tb * P:(tb + 1) * P], src[:, c, tb * P:(tb + 1) * P], w[:, c],
                                           start=c == 0, stop=c == DC - 1)
                            if c == 0 and tb == 0:
                                mm.then_inc(sem["tile_started"], 1)
                done(mm, name)

            def mods(first, count):
                j0 = len(order_of_tiles)
                order_of_tiles.extend(range(first, first + count))
                with pe.Fori(0, count // WR) as i:
                    for r in range(WR):
                        slot = (j0 + r) % WR
                        pe.wait_ge(w_ready[slot], i * 16 + 16 * ((j0 + r) // WR + 1))
                        for c in range(DC):
                            mm = pe.matmul(banks[3][:, bass.ds(i * WR + (first + r), 1)], wring[:, slot, c],
                                           col[:, COL_C + c:COL_C + c + 1], start=c == 0, stop=c == DC - 1)
                            if c == 0:
                                mm.then_inc(sem["tile_started"], 1)
                        mm.then_inc(sem["mod_tiles"], 1)

            def mod_batch(name, first, count):
                bank(name, 3)
                mods(first, count)
                position[name] = begun[0]

            def adaln(key):
                n = LN[key]
                fill_gap(1)
                pe.wait_ge(sem["sq_ready"], n + 1)
                b = bank(f"ms{n}", 0)
                for c in range(DC):
                    mm = pe.matmul(b[:, 0:HALF], ones, hT[:, c], start=c == 0, stop=c == DC - 1)
                done(mm, f"ms{n}")
                fill_gap(2)
                pe.wait_ge(sem["h_ready"], DC * (n + 1))

            def gla(key):
                g = key[2]
                adaln(key)
                if g == 0:
                    pe.wait_ge(sem["small_loaded"], 32)
                b = bank(f"glow{g}", 0)
                for c in range(DC):
                    mm = pe.matmul(b[0:RANK, 0:HALF], wsmall[:, 0, c], hT[:, c], start=c == 0, stop=c == DC - 1)
                done(mm, f"glow{g}")
                t0 = TILES["gla_in"]
                project(t0, f"q{g}.0", hT)
                taken(pe, f"glow{g}")
                for i in range(2):
                    b = bank(f"gate{g}.{i}", 1 + i)
                    for h in (2 * i, 2 * i + 1):
                        mm = pe.matmul(b[:, (h % 2) * HALF:(h % 2 + 1) * HALF], wg2[:, h * P:(h + 1) * P],
                                       g_low, start=True, stop=True)
                    done(mm, f"gate{g}.{i}")
                for h in range(1, GLA_H):
                    project(t0 + h, f"q{g}.{h}", hT)
                for h in range(GLA_H):
                    project(t0 + 4 + h, f"k{g}.{h}", hT)
                rest = [(t0 + 16 + c, f"g{g}.{c}", False) for c in range(DC)]
                rest += [(t0 + 8 + c, f"v{g}.{c}", True) for c in range(DC)]
                if g == 1:
                    bank("mod.2", 3)
                for lev in range(8):
                    if g == 1:
                        weave(7.0)
                        mods(48 + 8 * lev, 8)
                        position["mod.2"] = begun[0]
                    for w, name, tm in rest[2 * lev:2 * lev + 2]:
                        project(w, name, hT, tm)
                    if lev < 7:
                        pe.wait_ge(sem["ql_ready"], 8 * g + lev + 1)
                        pe.wait_ge(sem["kl_ready"], 8 * g + lev + 1)
                        ql, kl = g_ql, g_kl
                    else:
                        taken(pe, f"k{g}.3")
                        ql, kl = g_q, g_k
                    for tb in range(TBH):
                        ts = slice(tb * P, (tb + 1) * P)
                        b = bank(f"lev{g}.{lev}.{tb}", tb)
                        for h in range(GLA_H):
                            mm = pe.matmul(b[:, h * P:(h + 1) * P], kl[:, h, ts], ql[:, h, ts], start=True, stop=True)
                        done(mm, f"lev{g}.{lev}.{tb}")
                    weave(1.8)
                pe.wait_ge(sem["kl_ready"], 8 * (g + 1))
                for tb in range(TBH):
                    b = bank(f"kd{g}.{tb}", tb)
                    for h in range(GLA_H):
                        mm = pe.transpose(b[:, h * P:(h + 1) * P], g_kl[:, h, tb * P:(tb + 1) * P], ident)
                    done(mm, f"kd{g}.{tb}")
                pe.wait_ge(sem["attn_ready"], g + 1)
                taken(pe, f"v{g}.7")
                pe.wait_ge(sem["ql_ready"], 8 * (g + 1))
                for tb in range(TBH):
                    block_no = TBH * g + tb
                    ts = slice(tb * P, (tb + 1) * P)
                    if block_no:
                        pe.wait_ge(sem["state_ready"], block_no)
                    for half in range(2):
                        name = f"o{g}.{tb}.{half}"
                        b = bank(name, 2 + half)
                        for i in range(4):
                            h, vc = (4 * half + i) // 2, (4 * half + i) % 2
                            o = b[:, i * P:(i + 1) * P]
                            mm = pe.matmul(o, g_v[:, tb, (4 * half + i) * P:(4 * half + i + 1) * P],
                                           g_attn[:, tb, h], start=True, stop=block_no == 0)
                            if block_no:
                                mm = pe.matmul(o, g_state[:, h, vc * P:(vc + 1) * P], g_ql[:, h, ts],
                                               start=False, stop=True)
                        done(mm, name)
                    if block_no < NHALF * TBH - 1:
                        taken(pe, f"kd{g}.{tb}")
                        for half in range(2):
                            name = f"st{g}.{tb}.{half}"
                            b = bank(name, half)
                            for h in (2 * half, 2 * half + 1):
                                mm = pe.matmul(b[:, (h % 2) * GLA_HV:(h % 2 + 1) * GLA_HV], g_kd[:, tb, h],
                                               g_v[:, tb, h * GLA_HV:(h + 1) * GLA_HV], start=True, stop=True)
                            done(mm, name)
                if g == 0:
                    mod_batch("mod.1", 16, 32)
                fill_gap(1)
                pe.wait_ge(sem["sqo_ready"], g + 1)
                for half in range(2):
                    name = f"mso{g}.{half}"
                    b = bank(name, half)
                    for h in (2 * half, 2 * half + 1):
                        for vc in range(2):
                            mm = pe.matmul(b[:, (h % 2) * HALF:(h % 2 + 1) * HALF], ones, g_sq[:, 2 * h + vc],
                                           start=vc == 0, stop=vc == 1)
                    done(mm, name)
                fill_gap(3)
                pe.wait_ge(sem["o_ready"], 2 * (g + 1))
                for c in range(DC):
                    project(TILES["gla_out"] + c, f"mix0{g}.{c}", g_o)

            def route(key):
                l, hf = key[1:]
                r = RT[l, hf]
                adaln(key)
                for b4 in range(4):
                    name = f"htok{r}.{b4}"
                    b = bank(name, b4)
                    tb, half = b4 // 2, b4 % 2
                    for i in range(4):
                        mm = pe.transpose(b[:, i * P:(i + 1) * P], hT[:, half * 4 + i, tb * P:(tb + 1) * P], ident)
                    done(mm, name)
                for j in range(HP):
                    project(TILES[f"pq{l}"] + j, f"pq{r}.{j}", hT)
                fill_gap(1)
                taken(pe, f"pq{r}.{HP - 1}")
                for tb in range(TBH):
                    for kt in range(2):
                        w, _ = tile(TILES[f"keys{l}"] + kt)
                        for half in range(2):
                            name = f"s{r}.{tb}.{2 * kt + half}"
                            b = bank(name, 2 * kt + half)
                            for i in range(4):
                                mm = pe.matmul(b[:, i * P:(i + 1) * P],
                                               r_q[:, kt * 8 + half * 4 + i, tb * P:(tb + 1) * P],
                                               w[:, half * 4 + i], start=True, stop=True)
                                if half == 0 and i == 0:
                                    mm.then_inc(sem["tile_started"], 1)
                            done(mm, name)

            def gather(q):
                for b in range(TBH * q, TBH * q + TBH):
                    open_sums(b)
                    with pe.Fori(0, NSEL // NSLOT) as i:
                        for r in range(NSLOT):
                            pe.wait_ge(sem["diag_ready"], i * NSLOT + (b * NSEL + r + 1))
                            sum_rows(r)
                    close_sums(b)

            def fox(key):
                hf = key[2]
                adaln(key)
                pe.wait_ge(sem["hk_ready"], DC * (hf + 1))
                b = bank(f"f{hf}", 1)
                for c in range(DC):
                    mm = pe.matmul(b[0:FOX_H, 0:HALF], wsmall[:, 1, c], f_hk[:, c], start=c == 0, stop=c == DC - 1)
                done(mm, f"f{hf}")

                def norm(what, i, sq_no):
                    pe.wait_ge(sem["fsq_ready"], 4 * hf + sq_no + 1)
                    for half in range(2):
                        name = f"fms{hf}.{what}{i}.{half}"
                        b = bank(name, 2 + half)
                        for m in range(2):
                            mm = pe.matmul(b[:, m * HALF:(m + 1) * HALF], blockdiag, f_sq[:, 2 * half + m],
                                           start=True, stop=True)
                        done(mm, name)

                for c in range(DC):
                    project(TILES["fox_kv"] + c, f"fk{hf}.{c}", f_hk)
                for c in range(DC):
                    project(TILES["fox_kv"] + DC + c, f"fv{hf}.{c}", f_hk, True)
                    if c in (3, 7):
                        norm("k", c // 4, c // 4)
                for c in range(DC):
                    project(TILES["fox_qg"] + c, f"fq{hf}.{c}", hT)
                for c in range(DC):
                    project(TILES["fox_qg"] + DC + c, f"fg{hf}.{c}", hT)
                    if c in (3, 7):
                        norm("q", c // 4, 2 + c // 4)
                pe.wait_ge(sem["fn_ready"], 4 * (hf + 1))
                pe.wait_ge(sem["cum_ready"], hf + 1)
                taken(pe, f"fv{hf}.{DC - 1}")

                units = [(tb, h) for tb in range(TBH) for h in range(FOX_H)]

                def scores(u):
                    tb, h = units[u]
                    keys = (TBH * hf + tb + 1) * P
                    pb, c, ts = FOX_HD * (h % 2), h // 2, slice(tb * P, (tb + 1) * P)
                    b = bank(f"sc{hf}.{u}", u % 2)
                    pe.matmul(b[:, 0:keys], f_q[pb:pb + FOX_HD, c, ts], f_k[pb:pb + FOX_HD, c, 0:keys],
                              start=True, stop=False)
                    pe.matmul(b[:, 0:keys], ident[0:FOX_H, h:h + 1].to_broadcast([FOX_H, P]), ncum[:, 0:keys],
                              start=False, stop=False)
                    mm = pe.matmul(b[:, keys - P:keys], ident, negmask, start=False, stop=True)
                    done(mm, f"sc{hf}.{u}")

                def turn(u):
                    tb, h = units[u]
                    pe.wait_ge(sem["pn_ready"], len(units) * hf + u + 1)
                    b = bank(f"pt{hf}.{u}", 2)
                    for kb in range(TBH * hf + tb + 1):
                        mm = pe.transpose(b[:, kb * P:(kb + 1) * P], f_p[:, u % 2, kb * P:(kb + 1) * P], ident)
                    done(mm, f"pt{hf}.{u}")

                def mix(u):
                    tb, h = units[u]
                    taken(pe, f"pt{hf}.{u}")
                    name = f"fo{hf}.{tb}.{h // 8}"
                    b = bank(name, 3) if h % 8 == 0 else banks[3]
                    pb, c = FOX_HD * (h % 2), (h // 2) % 4
                    for kb in range(TBH * hf + tb + 1):
                        mm = pe.matmul(b[pb:pb + FOX_HD, c * P:(c + 1) * P], f_v[:, kb, h * FOX_HD:(h + 1) * FOX_HD],
                                       f_pt[:, u % 2, kb * P:(kb + 1) * P], start=kb == 0,
                                       stop=kb == TBH * hf + tb)
                    mm.then_inc(sem["mixed"], 1)
                    position[f"mix{hf}.{u}"] = begun[0]

                scores(0)
                for u in range(len(units) + 1):
                    if u + 1 < len(units):
                        scores(u + 1)
                    weave(1.0)
                    if u < len(units):
                        turn(u)
                    weave(1.0)
                    if u:
                        mix(u - 1)
                    weave(0.9)
                fill_gap(1)
                pe.wait_ge(sem["fgated"], hf + 1)
                for c in range(DC):
                    project(TILES["fox_out"] + c, f"mix1{hf}.{c}", f_o)

            pe.wait_ge(sem["const_loaded"], 16)
            pe.wait_ge(sem["col_loaded"], 16)
            mod_batch("mod.0", 0, 16)
            for q, stages in PLAN:
                open_window(q)
                pace[0] = {0: 3.0, 1: 3.6, 2: 3.6}.get(q, 3.0)
                if q is not None and not stages:
                    gather(q)
                for key in stages:
                    {"gla": gla, "route": route, "fox": fox}[key[0]](key)
                    if key[0] == "route":
                        while begun[0] < window[1]:
                            step(begun[0])

        @block.sync
        def _(sp):
            keep_up[sp.engine] = lambda x: None
            open_window(None)
            sp.dma_start(col[:], cols).then_inc(sem["col_loaded"], 16)
            sp.dma_start(const[:], consts).then_inc(sem["const_loaded"], 16)
            sp.dma_start(view(tmp, 7168, 8 * P), masks).then_inc(sem["mask_loaded"], 16)
            sp.dma_start(xT[:], xt.rearrange("(c p) t -> p c t", p=P)).then_inc(sem["x_loaded"], 16)
            sp.dma_start(wsmall[:].rearrange("p a c n -> p (a c n)"), small).then_inc(sem["small_loaded"], 16)
            sp.dma_start(wg2[:], wgate).then_inc(sem["small_loaded"], 16)
            at = 0
            while at < len(order_of_tiles):
                n = 1
                while at + n < len(order_of_tiles) and order_of_tiles[at + n] == order_of_tiles[at] + n:
                    n += 1
                first = order_of_tiles[at]
                if at == 0 or n < 2 * WR or at % WR:
                    head = min(n, WR) if at == 0 else (n if n < 2 * WR else (-at) % WR)
                    for j in range(at, at + head):
                        if j >= WR:
                            sp.wait_ge(sem["tile_started"], j - WR + 2)
                        sp.dma_start(wring[:, j % WR], wt[order_of_tiles[j]]).then_inc(w_ready[j % WR], 16)
                    at += head
                    continue
                with sp.Fori(0, n // WR) as i:
                    for r in range(WR):
                        sp.wait_ge(sem["tile_started"], i * WR + (at + r - WR + 2))
                        sp.dma_start(wring[:, r], wt[bass.ds(i * WR + (first + r), 1)].rearrange("o p c n -> (o p) c n"))\
                            .then_inc(w_ready[r], 16)
                at += n // WR * WR
            for hf in range(NHALF):
                sp.wait_ge(x_ffn[1][hf], DC * TBH)
                sp.dma_start(out.rearrange("(c p) t -> p c t", p=P)[:, :, hf * HALF:(hf + 1) * HALF],
                             xT[:, :, hf * HALF:(hf + 1) * HALF]).then_inc(sem["out_written"], 16)
            sp.wait_ge(sem["out_written"], 32)

        def half_of(hf):
            return slice(hf * HALF, (hf + 1) * HALF)

        @block.vector
        def _(dve):
            chain = [0]

            def mark(ins):
                chain[0] += 1
                ins.then_inc(sem["dve_chain"], 1)

            def settle():
                dve.wait_ge(sem["dve_chain"], chain[0])

            def link(ins):
                mark(ins)
                settle()

            def mod_batch(name, first, count, tiles):
                catch_up(position[name])
                dve.wait_ge(sem["mod_tiles"], tiles)
                at = slice(first, first + count)
                mark(dve.tensor_tensor(mod[:, at], banks[3][:, at], col[:, COL_MODB + first:COL_MODB + first + count],
                                       ALU.add))
                settle()
                link(dve.tensor_scalar(mod1[:, at], mod[:, at], 1.0, None, ALU.add))

            def adaln(key):
                kind, l, hf = key
                n = LN[key]
                full(dve, f"ms{n}")
                freed(dve.tensor_scalar(rms[:], bank_of(f"ms{n}")[:, 0:HALF], 1.0 / D, EPS, ALU.mult, ALU.add), f"ms{n}")
                taken(dve, f"ms{n}")
                dve.sem_inc(sem["ms_ready"], 1)
                dve.wait_ge(sem["rms_ready"], n + 1)
                link(dve.reciprocal(rms[:], rms[:]))
                dve.tensor_tensor(hT[:], xT[:, :, half_of(hf)],
                                  rms[:].rearrange("p (o t) -> p o t", o=1).to_broadcast([P, DC, HALF]),
                                  ALU.mult).then_inc(sem["xn_ready"], 1)

            def add_residual(l, hf, names, gate_at, signal):
                for c in range(DC):
                    full(dve, names[c])
                    x = xT[:, c, half_of(hf)]
                    freed(dve.scalar_tensor_tensor(x, bank_of(names[c])[:, 0:HALF], mod[:, gate_at + c:gate_at + c + 1],
                                                   x, ALU.mult, ALU.add), names[c])
                dve.drain().then_inc(signal, DC)

            dotted, weighed, added, here, credit = [0], [0], [0], [0], [0.0]

            def begin(q):
                dve.wait_ge(sem["route_ready"], TBH * (q + 1))
                b, n, _ = fills[f"htok{q}.3"]
                dve.wait_ge(bank_taken[b], n)

            def dot(r, q, tb):
                u = ring[:, r, 0:D]
                dve.tensor_tensor_reduce(u, u, htok[:, q % 2, tb], 1.0, 0.0, ALU.mult, ALU.add,
                                         dots[:, r:r + 1]).then_inc(sem["dot_ready"], 1)

            def weigh(r, gate_of):
                dve.tensor_scalar(diag[:, r], ident, acts[:, r:r + 1], gate_of, ALU.mult, ALU.mult)\
                   .then_inc(sem["diag_ready"], 1)

            def add_block(b):
                l, hf = GATHER[b // TBH]
                tb = b % TBH
                dve.wait_ge(sem["acc_full"], 2 * b + 2)
                for c in range(DC):
                    at = hf * HALF + tb * P
                    x = xT[:, c, at:at + P]
                    ins = dve.scalar_tensor_tensor(x, acc[:, c // 4, (c % 4) * P:(c % 4 + 1) * P],
                                                   mod[:, 48 * l + 40 + c:48 * l + 41 + c], x, ALU.mult, ALU.add)
                    if c < DC - 1:
                        ins.then_inc(x_ffn[l][hf], 1)
                ins.then_inc(sem["acc_free"], 1)
                dve.wait_ge(sem["acc_free"], b + 1)
                dve.sem_inc(x_ffn[l][hf], 1)
                if tb == TBH - 1:
                    dve.sem_inc(sem["dots_done"], 1)

            def catch_up(x):
                for at in range(here[0], min(x, window[1]) + 1):
                    here[0] = at
                    keep_step(at)

            def keep_step(x):
                while dotted[0] < min(x + 2, window[1]) or weighed[0] < min(x + 1, window[1]):
                    s = dotted[0]
                    if s < min(x + 2, window[1]):
                        dotted[0] += 1
                        if s % HALF_STEPS == 0:
                            begin(s // HALF_STEPS)
                        b = s // BLOCK_STEPS
                        for k in range(PAIR * s, PAIR * s + PAIR):
                            r = k % NSLOT
                            dve.wait_ge(row_ready[r], 16 * (k // NSLOT + 1))
                            dot(r, b // TBH, b % TBH)
                    w = weighed[0]
                    if w < min(x + 1, window[1]) and (w < dotted[0] - 1 or dotted[0] == window[1]
                                                      or dotted[0] >= min(x + 2, window[1])):
                        weighed[0] += 1
                        b = w // BLOCK_STEPS
                        dve.wait_ge(sem["gelu_ready"], w + 1)
                        for k in range(PAIR * w, PAIR * w + PAIR):
                            at = k - b * NSEL + b % TBH * NSEL
                            weigh(k % NSLOT, gate[:, b // TBH % 2, at:at + 1])
                while added[0] < x // BLOCK_STEPS:
                    added[0] += 1
                    add_block(added[0] - 1)

            def work(us):
                credit[0] += us
                while credit[0] >= 3.2:
                    credit[0] -= 3.2
                    catch_up(here[0] + 1)

            def told(name, n):
                position[name, n] = here[0]

            keep_up[dve.engine] = catch_up
            open_window(None)

            def log_sigmoid_first(z, a, signal):
                dve.scalar_tensor_tensor(a, z, -1.0, z, ALU.mult, ALU.min).then_inc(signal, 1)

            def log_sigmoid_last(z, a):
                link(dve.scalar_tensor_tensor(z, z, 0.0, a, ALU.min, ALU.subtract))

            def gla(key):
                g = key[2]
                adaln(key)
                if g == 0:
                    dve.wait_ge(sem["mask_loaded"], 16)
                    link(dve.tensor_copy(levmask[:], view(tmp, 7168, 8, P)))
                link(dve.memset(g_attn, 0.0))
                d3 = g_d.rearrange("p (a b) -> p a b", a=GLA_H)
                for i in range(2):
                    name = f"gate{g}.{i}"
                    full(dve, name)
                    b = bank_of(name)
                    for h in (2 * i, 2 * i + 1):
                        ins = dve.tensor_scalar(d3[:, h], b[:, (h % 2) * HALF:(h % 2 + 1) * HALF],
                                                col[:, COL_BG + h:COL_BG + h + 1], None, ALU.add)
                    freed(ins, name)
                    taken(dve, name)
                log_sigmoid_first(g_d, g_e, sem["gate_abs"])
                dve.wait_ge(sem["gate_soft"], g + 1)
                log_sigmoid_last(g_d, g_e)
                for i in range(GLA_H * TBH):
                    ts = slice(i * P, (i + 1) * P)
                    mark(dve.tensor_tensor_scan(g_b[:, ts], ones, g_d[:, ts], 0.0, ALU.mult, ALU.add))
                settle()

                def keep(lev):
                    for tb in range(TBH):
                        name = f"lev{g}.{lev}.{tb}"
                        full(dve, name)
                        m = levmask[:, lev].rearrange("p (o b) -> p o b", o=1).to_broadcast([P, GLA_H, P])
                        freed(dve.copy_predicated(g_attn[:, tb], m, bank_of(name)[:].rearrange("p (a b) -> p a b", a=GLA_H)),
                              name)

                for lev, half in enumerate(LEVELS):
                    nb = GLA_H * HALF // (2 * half)
                    bv = g_b.rearrange("p (n t) -> p n t", n=nb)
                    dv = g_d.rearrange("p (n t) -> p n t", n=nb)
                    link(dve.tensor_tensor(dv, bv, bv[:, :, half - 1:half].to_broadcast([P, nb, 2 * half]), ALU.subtract))
                    if lev:
                        dve.wait_ge(sem["kl_ready"], 8 * g + lev)
                    dve.scalar_tensor_tensor(g_e, g_d, -1.0, g_d, ALU.mult, ALU.min).then_inc(sem["level_gap"], 1)
                    if lev:
                        keep(lev - 1)
                    if lev == 0:
                        taken(dve, f"k{g}.3")
                    dve.wait_ge(sem["level_exp"], 7 * g + lev + 1)
                    dve.tensor_tensor(g_ql, g_q, g_e.rearrange("p (a b) -> p a b", a=GLA_H), ALU.mult)\
                       .then_inc(sem["ql_ready"], 1)
                bv = g_b.rearrange("p (n t) -> p n t", n=GLA_H * TBH)
                dve.wait_ge(sem["kl_ready"], 8 * g + 7)
                dve.wait_ge(sem["ql_ready"], 8 * g + 7)
                dve.tensor_tensor(g_e.rearrange("p (n t) -> p n t", n=GLA_H * TBH),
                                  bv[:, :, P - 1:P].to_broadcast([P, GLA_H * TBH, P]), bv, ALU.subtract)\
                   .then_inc(sem["last_gap"], 1)
                keep(6)
                keep(7)
                dve.drain().then_inc(sem["attn_ready"], 1)
                if g == 1:
                    mod_batch("mod.2", 48, 64, NMOD)
                    dve.drain().then_inc(sem["mods_ready"], 1)
                    dve.sem_inc(bank_taken[3], 1)
                dve.wait_ge(sem["chunk_exp"], g + 1)
                mark(dve.tensor_copy(g_el.rearrange("p (n o) -> p n o", o=1),
                                     g_d.rearrange("p (n t) -> p n t", n=GLA_H * TBH)[:, :, P - 1:P]))
                dve.tensor_tensor(g_ql, g_q, d3, ALU.mult).then_inc(sem["ql_ready"], 1)
                settle()
                for tb in range(TBH):
                    block_no = TBH * g + tb
                    if block_no == NHALF * TBH - 1:
                        break
                    for half in range(2):
                        name = f"st{g}.{tb}.{half}"
                        full(dve, name)
                        for h in (2 * half, 2 * half + 1):
                            new = bank_of(name)[:, (h % 2) * GLA_HV:(h % 2 + 1) * GLA_HV]
                            if block_no == 0:
                                ins = dve.tensor_copy(g_state[:, h], new)
                            else:
                                ins = dve.scalar_tensor_tensor(g_state[:, h], g_state[:, h],
                                                               g_el[:, h * TBH + tb:h * TBH + tb + 1], new,
                                                               ALU.mult, ALU.add)
                        freed(ins, name)
                    taken(dve, f"st{g}.{tb}.1")
                    dve.sem_inc(sem["state_ready"], 1)
                if g == 0:
                    mod_batch("mod.1", 16, 32, 48)
                    dve.drain().then_inc(sem["mods_ready"], 1)
                    dve.sem_inc(bank_taken[3], 1)
                for half in range(2):
                    name = f"mso{g}.{half}"
                    full(dve, name)
                    freed(dve.tensor_scalar(g_rs[:, 2 * half:2 * half + 2], bank_of(name)[:].rearrange("p (a b) -> p a b", a=2),
                                            1.0 / GLA_HV, EPS, ALU.mult, ALU.add), name)
                dve.drain().then_inc(sem["mso_ready"], 1)
                dve.wait_ge(sem["rmso_ready"], g + 1)
                link(dve.reciprocal(g_rs, g_rs))
                ov = g_o.rearrange("p (h v) t -> p h v t", h=GLA_H)
                sv = g_sq.rearrange("p (h v) t -> p h v t", h=GLA_H)
                for vc in range(2):
                    mark(dve.tensor_tensor(ov[:, :, vc], ov[:, :, vc], g_rs, ALU.mult))
                dve.wait_ge(sem["silu_exp"], g + 1)
                link(dve.tensor_scalar(g_sq, g_sq, 1.0, None, ALU.add))
                link(dve.reciprocal(g_sq, g_sq))
                link(dve.tensor_tensor(g_sq, g_sq, g_g, ALU.mult))
                for vc in range(2):
                    dve.scalar_tensor_tensor(ov[:, :, vc], ov[:, :, vc], col[:, COL_ON + vc:COL_ON + vc + 1],
                                             sv[:, :, vc], ALU.mult, ALU.mult).then_inc(sem["o_ready"], 1)
                add_residual(0, g, [f"mix0{g}.{c}" for c in range(DC)], 16, x_mix[0][g])

            def top16(values, indices, src):
                n = src.shape[1]
                us = 0.06 + src.shape[2] / 960.0
                for i in range(n):
                    mark(dve.max(values[:, i, 0:8], src[:, i]))
                    work(us)
                settle()
                for i in range(n):
                    mark(dve.max_index(indices[:, i, 0:8], values[:, i, 0:8], src[:, i]))
                    work(us)
                for i in range(n):
                    mark(dve.match_replace(src[:, i], values[:, i, 0:8], src[:, i], NEG))
                    work(us)
                settle()
                for i in range(n):
                    mark(dve.max(values[:, i, 8:16], src[:, i]))
                    work(us)
                settle()
                for i in range(n):
                    mark(dve.max_index(indices[:, i, 8:16], values[:, i, 8:16], src[:, i]))
                    work(us)
                settle()

            def route(key):
                l, hf = key[1:]
                r = RT[l, hf]
                adaln(key)
                for tb in range(TBH):
                    taken(dve, f"s{r}.{tb}.3")
                    top16(r_v, r_i, r_s)
                    mark(dve.tensor_copy(r_if, r_i))
                    halves = r_v.rearrange("p (h s) k -> p h s k", s=2)
                    link(dve.tensor_tensor(r_cand.rearrange("p h (a b) -> p h a b", a=TOPK),
                                           halves[:, :, 0].unsqueeze(3).to_broadcast([P, PH, TOPK, TOPK]),
                                           halves[:, :, 1].unsqueeze(2).to_broadcast([P, PH, TOPK, TOPK]), ALU.add))
                    top16(r_ts, r_tc, r_cand)
                    mark(dve.tensor_copy(r_max.unsqueeze(2), r_ts[:, :, 0:1]))
                    settle()
                    dve.tensor_tensor(r_ts, r_ts, r_max.unsqueeze(2).to_broadcast([P, PH, TOPK]), ALU.subtract)\
                       .then_inc(sem["top_ready"], 1)
                    told("top_ready", TBH * r + tb + 1)
                    for side in range(2):
                        tc = r_tc.rearrange("p a b -> p (a b)")
                        if side == 0:
                            link(dve.tensor_scalar(r_hu, tc, 4, None, ALU.logical_shift_right))
                        else:
                            link(dve.tensor_scalar(r_hu, tc, TOPK - 1, None, ALU.bitwise_and))
                        link(dve.tensor_copy(r_hf, r_hu))
                        link(dve.tensor_tensor(r_hot, r_hf.unsqueeze(2).to_broadcast([P, NSEL, TOPK]),
                                               iota.unsqueeze(1).to_broadcast([P, NSEL, TOPK]), ALU.is_equal))
                        hot = r_hot.rearrange("p (h k) a -> p h k a", h=PH)
                        names = r_if.rearrange("p (h s) k -> p h s k", s=2)[:, :, side]
                        link(dve.tensor_tensor(hot, hot, names.unsqueeze(2).to_broadcast([P, PH, TOPK, TOPK]), ALU.mult))
                        work(5.0)
                        mark(dve.tensor_reduce(r_sel[:, side], r_hot, AX_X, ALU.add))
                        work(2.3)
                    settle()
                    if r >= 2:
                        dve.wait_ge(sem["acc_full"], 2 * TBH * (r - 1))
                    mine = slice(tb * NSEL, (tb + 1) * NSEL)
                    link(dve.scalar_tensor_tensor(r_hf, r_sel[:, 0], float(NK), r_sel[:, 1], ALU.mult, ALU.add))
                    mark(dve.tensor_scalar(idx[:, r % 2, mine], r_hf, float(l * EXPERTS), None, ALU.add))
                    dve.wait_ge(sem["top_exp"], TBH * r + tb + 1)
                    link(dve.tensor_reduce(r_sum, r_ts, AX_X, ALU.add))
                    link(dve.reciprocal(r_sum, r_sum))
                    dve.tensor_tensor(gate[:, r % 2, mine].rearrange("p (h k) -> p h k", h=PH), r_ts,
                                      r_sum.unsqueeze(2).to_broadcast([P, PH, TOPK]), ALU.mult)\
                       .then_inc(sem["route_ready"], 1)
                    dve.drain().then_inc(sem["s_free"], 1)
                    told("s_free", TBH * r + tb + 1)

            def gather(q):
                begin(q)
                l, hf = GATHER[q]
                for tb in range(TBH):
                    b = TBH * q + tb
                    with dve.Fori(0, NSEL // NSLOT) as i:
                        for pr in range(NSLOT // PAIR):
                            for r in range(PAIR * pr, PAIR * pr + PAIR):
                                dve.wait_ge(row_ready[r], i * 16 + 16 * (b * NSEL // NSLOT + 1))
                                dot(r, q, tb)
                            dve.wait_ge(sem["gelu_ready"], i * (NSLOT // PAIR) + (b * NSEL // PAIR + pr + 1))
                            for r in range(PAIR * pr, PAIR * pr + PAIR):
                                weigh(r, gate[:, q % 2, bass.ds(i * NSLOT + (tb * NSEL + r), 1)])
                    add_block(b)

            def fox(key):
                hf = key[2]
                if hf == 0:
                    link(dve.tensor_scalar(qn8[:], col[:, COL_QN:COL_QN + 1], FOX_HD ** -0.5, None, ALU.mult))
                adaln(key)
                name = f"f{hf}"
                full(dve, name)
                freed(dve.tensor_scalar(f_z, bank_of(name)[0:FOX_H, 0:HALF], col[0:FOX_H, COL_BF:COL_BF + 1], None,
                                        ALU.add), name)
                taken(dve, name)
                log_sigmoid_first(f_z, f_a, sem["fgate_abs"])
                dve.wait_ge(sem["fgate_soft"], hf + 1)
                link(dve.scalar_tensor_tensor(f_z, f_z, 0.0, f_a, ALU.min, ALU.subtract))
                at = hf * HALF
                one_row = ones[0:FOX_H, 0:1].to_broadcast([FOX_H, HALF])
                dve.tensor_tensor_scan(ncum[:, at:at + HALF], one_row, f_z,
                                       ncum[:, at - 1:at] if hf else 0.0, ALU.mult, ALU.subtract)\
                   .then_inc(sem["cum_ready"], 1)

                def norm(x, what, i, sq_no, gain):
                    if 4 * hf + sq_no:
                        dve.wait_ge(sem["fn_ready"], 4 * hf + sq_no)
                    for half in range(2):
                        name = f"fms{hf}.{what}{i}.{half}"
                        full(dve, name)
                        freed(dve.tensor_scalar(f_rs[:, 2 * half:2 * half + 2], bank_of(name)[:].rearrange("p (a b) -> p a b", a=2),
                                                1.0 / FOX_HD, EPS, ALU.mult, ALU.add), name)
                    dve.drain().then_inc(sem["fms_ready"], 1)
                    dve.wait_ge(sem["frms_ready"], 4 * hf + sq_no + 1)
                    link(dve.reciprocal(f_rs, f_rs))
                    dve.scalar_tensor_tensor(x, x, gain, f_rs, ALU.mult, ALU.mult).then_inc(sem["fn_ready"], 1)

                for i in range(2):
                    norm(f_k[:, 4 * i:4 * i + 4, half_of(hf)], "k", i, i, col[:, COL_KN:COL_KN + 1])
                for i in range(2):
                    norm(f_q[:, 4 * i:4 * i + 4], "q", i, 2 + i, qn8[:, 0:1])
                nu = TBH * FOX_H

                def negmax(u):
                    keys = (TBH * hf + u // FOX_H + 1) * P
                    name = f"sc{hf}.{u}"
                    full(dve, name)
                    dve.tensor_reduce(f_nm[:, u % 2:u % 2 + 1], bank_of(name)[:, 0:keys], AX_X, ALU.max, negate=True)\
                       .then_inc(sem["negmax_ready"], 1)

                negmax(0)
                for u in range(nu):
                    keys = (TBH * hf + u // FOX_H + 1) * P
                    if u + 1 < nu:
                        negmax(u + 1)
                    dve.wait_ge(sem["p_ready"], nu * hf + u + 1)
                    at = slice(u % 2, u % 2 + 1)
                    freed(dve.reciprocal(f_inv[:, at], f_sum[:, at]), f"sc{hf}.{u}")
                    taken(dve, f"sc{hf}.{u}")
                    p = f_p[:, u % 2, 0:keys]
                    dve.tensor_scalar(p, p, f_inv[:, at], None, ALU.mult).then_inc(sem["pn_ready"], 1)
                catch_up(position[f"mix{hf}.{nu - 1}"])
                dve.wait_ge(sem["fsig_exp"], hf + 1)
                link(dve.tensor_scalar(f_e, f_e, 1.0, None, ALU.add))
                link(dve.reciprocal(f_e, f_e))
                dve.tensor_tensor(f_o, f_o, f_e, ALU.mult).then_inc(sem["fgated"], 1)
                add_residual(1, hf, [f"mix1{hf}.{c}" for c in range(DC)], 64, x_mix[1][hf])

            dve.wait_ge(sem["col_loaded"], 16)
            dve.wait_ge(sem["const_loaded"], 16)
            mod_batch("mod.0", 0, 16, 16)
            dve.drain().then_inc(sem["mods_ready"], 1)
            dve.sem_inc(bank_taken[3], 1)
            for q, stages in PLAN:
                open_window(q)
                if q is not None and not stages:
                    gather(q)
                for key in stages:
                    {"gla": gla, "route": route, "fox": fox}[key[0]](key)
                    if key[0] == "route":
                        catch_up(window[1])

        @block.scalar
        def _(act):
            chain = [0]

            def link(ins):
                chain[0] += 1
                ins.then_inc(sem["act_chain"], 1)
                act.wait_ge(sem["act_chain"], chain[0])

            activated, summed, here = [0], [0], [0]

            def take_sums(b):
                act.wait_ge(sem["acc_full"], 2 * b + 1)
                act.activation(htok[:, b // TBH % 2, b % TBH], acc[:].rearrange("p a b -> p (a b)"), ACT.Copy)\
                   .then_inc(sem["otok_ready"], 1)

            def catch_up(x):
                for at in range(here[0], min(x, window[1]) + 1):
                    here[0] = at
                    keep_step(at)

            def keep_step(x):
                while activated[0] < min(x + 1, window[1]):
                    s = activated[0]
                    activated[0] += 1
                    at = slice(PAIR * s % NSLOT, PAIR * s % NSLOT + PAIR)
                    act.wait_ge(sem["dot_ready"], PAIR * (s + 1))
                    act.activation(acts[:, at], dots[:, at], ACT.Gelu).then_inc(sem["gelu_ready"], 1)
                while summed[0] < x // BLOCK_STEPS:
                    take_sums(summed[0])
                    summed[0] += 1

            keep_up[act.engine] = catch_up
            open_window(None)

            def x_is_ready(key):
                kind, l, hf = key
                if kind == "gla":
                    act.wait_ge(sem["x_loaded"], 16)
                elif kind == "fox":
                    act.wait_ge(x_ffn[0][hf], DC * TBH)
                else:
                    catch_up(position[f"mix{l}{hf}.{DC - 1}"])
                    act.wait_ge(x_mix[l][hf], DC)

            def adaln(key):
                kind, l, hf = key
                n = LN[key]
                x_is_ready(key)
                if n:
                    prev = [k for k in LN if LN[k] == n - 1][0]
                    full(act, {"gla": f"v{prev[2]}.{DC - 1}", "route": f"pq{RT.get(prev[1:])}.{HP - 1}",
                               "fox": f"fg{prev[2]}.{DC - 1}"}[prev[0]])
                act.activation(hT[:], xT[:, :, half_of(hf)], ACT.Square).then_inc(sem["sq_ready"], 1)
                catch_up(position[f"ms{n}"])
                act.wait_ge(sem["ms_ready"], n + 1)
                act.activation(rms[:], rms[:], ACT.Sqrt).then_inc(sem["rms_ready"], 1)
                act.wait_ge(sem["xn_ready"], n + 1)
                act.wait_ge(sem["mods_ready"], 3 if l == 1 else (1 if kind == "gla" else 2))
                if kind == "fox":
                    for c in range(DC):
                        act.activation(f_hk[:, c], hT[:, c], ACT.Identity, bias=mod[:, 96 + c:97 + c],
                                       scale=mod1[:, 104 + c:105 + c]).then_inc(sem["hk_ready"], 1)
                base = 48 * l + (24 if kind == "route" else 0)
                for c in range(DC):
                    act.activation(hT[:, c], hT[:, c], ACT.Identity, bias=mod[:, base + c:base + c + 1],
                                   scale=mod1[:, base + 8 + c:base + 9 + c]).then_inc(sem["h_ready"], 1)

            def take(name, dst, scale=1.0, src=None):
                full(act, name)
                b = bank_of(name)[:]
                freed(act.activation(dst, src(b) if src else b, ACT.Copy, scale=scale), name)

            def left(b):
                return b[:, 0:HALF]

            def left2(b):
                return b[:, 0:HALF].rearrange("p (a b) -> p a b", a=TBH)

            def four(b):
                return b.rearrange("p (a b) -> p a b", a=4)

            def gla(key):
                g = key[2]
                adaln(key)
                take(f"glow{g}", g_low, src=lambda b: b[0:RANK, 0:HALF])
                take(f"q{g}.0", g_q[:, 0], GLA_HK ** -0.5, left)
                catch_up(position[f"gate{g}.1"])
                act.wait_ge(sem["gate_abs"], g + 1)
                link(act.activation(g_e, g_e, ACT.Exp))
                act.activation(g_e, g_e, ACT.Ln, bias=1.0).then_inc(sem["gate_soft"], 1)
                for h in range(1, GLA_H):
                    take(f"q{g}.{h}", g_q[:, h], GLA_HK ** -0.5, left)
                for h in range(GLA_H):
                    take(f"k{g}.{h}", g_k[:, h], 1.0, left)
                for lev in range(8):
                    if lev < 7:
                        act.wait_ge(sem["level_gap"], 7 * g + lev + 1)
                        act.activation(g_e, g_e, ACT.Exp, scale=1.0 / 16).then_inc(sem["level_exp"], 1)
                    for i in (2 * lev, 2 * lev + 1):
                        if i < DC:
                            take(f"g{g}.{i}", g_g[:, i], 1.0, left)
                        else:
                            c = i - DC
                            take(f"v{g}.{c}", g_v[:, :, c * P:(c + 1) * P], 1.0, left2)
                act.wait_ge(sem["last_gap"], g + 1)
                act.activation(g_e, g_e, ACT.Exp, scale=1.0 / 16).then_inc(sem["last_exp"], 1)
                act.activation(g_d, g_b, ACT.Exp, scale=1.0 / 16).then_inc(sem["chunk_exp"], 1)
                for tb in range(TBH):
                    take(f"kd{g}.{tb}", g_kd[:, tb], 1.0, four)
                for tb in range(TBH):
                    for half in range(2):
                        take(f"o{g}.{tb}.{half}", g_o[:, 4 * half:4 * half + 4, tb * P:(tb + 1) * P], 1.0, four)
                taken(act, f"o{g}.{TBH - 1}.1")
                act.wait_ge(sem["ql_ready"], 8 * (g + 1))
                act.wait_ge(sem["kl_ready"], 8 * (g + 1))
                act.activation(g_sq, g_o, ACT.Square).then_inc(sem["sqo_ready"], 1)
                catch_up(position[f"mso{g}.1"])
                act.wait_ge(sem["mso_ready"], g + 1)
                act.activation(g_rs, g_rs, ACT.Sqrt).then_inc(sem["rmso_ready"], 1)
                act.activation(g_sq, g_g, ACT.Exp, scale=-1.0).then_inc(sem["silu_exp"], 1)

            def route(key):
                r = RT[key[1:]]
                adaln(key)
                if r >= 2:
                    act.wait_ge(sem["dots_done"], r - 1)
                for b4 in range(4):
                    tb, half = b4 // 2, b4 % 2
                    take(f"htok{r}.{b4}", htok[:, r % 2, tb, half * 512:(half + 1) * 512])
                for j in range(HP):
                    take(f"pq{r}.{j}", r_q[:, j], 1.0, left)
                for tb in range(TBH):
                    n = TBH * r + tb
                    if tb:
                        catch_up(position["s_free", n])
                        act.wait_ge(sem["s_free"], n)
                    for b4 in range(4):
                        take(f"s{r}.{tb}.{b4}", r_s[:, 4 * b4:4 * b4 + 4], 1.0, four)
                    catch_up(position["top_ready", n + 1])
                    act.wait_ge(sem["top_ready"], n + 1)
                    act.activation(r_ts, r_ts, ACT.Exp).then_inc(sem["top_exp"], 1)

            def gather(q):
                for b in range(TBH * q, TBH * q + TBH):
                    with act.Fori(0, NSEL // NSLOT) as i:
                        for pr in range(NSLOT // PAIR):
                            at = slice(PAIR * pr, PAIR * pr + PAIR)
                            act.wait_ge(sem["dot_ready"], i * NSLOT + (b * NSEL + PAIR * pr + PAIR))
                            act.activation(acts[:, at], dots[:, at], ACT.Gelu).then_inc(sem["gelu_ready"], 1)
                    take_sums(b)

            def fox(key):
                hf = key[2]
                adaln(key)
                catch_up(position[f"f{hf}"])
                act.wait_ge(sem["fgate_abs"], hf + 1)
                link(act.activation(f_a, f_a, ACT.Exp))
                act.activation(f_a, f_a, ACT.Ln, bias=1.0).then_inc(sem["fgate_soft"], 1)

                def square(x, after):
                    taken(act, after)
                    act.activation(f_sq, x, ACT.Square).then_inc(sem["fsq_ready"], 1)

                def root(sq_no):
                    catch_up(position[f"fms{hf}.{'kkqq'[sq_no]}{sq_no % 2}.1"])
                    act.wait_ge(sem["fms_ready"], 4 * hf + sq_no + 1)
                    act.activation(f_rs, f_rs, ACT.Sqrt).then_inc(sem["frms_ready"], 1)

                for c in range(DC):
                    take(f"fk{hf}.{c}", f_k[:, c, half_of(hf)], 1.0, left)
                for i in range(2):
                    square(f_k[:, 4 * i:4 * i + 4, half_of(hf)], f"fk{hf}.{DC - 1}")
                    for c in range(4 * i, 4 * i + 4):
                        take(f"fv{hf}.{c}", f_v[:, TBH * hf:TBH * hf + TBH, c * P:(c + 1) * P], 1.0, left2)
                    root(i)
                for c in range(DC):
                    take(f"fq{hf}.{c}", f_q[:, c], 1.0, left)
                for i in range(2):
                    square(f_q[:, 4 * i:4 * i + 4], f"fq{hf}.{DC - 1}")
                    for c in range(4 * i, 4 * i + 4):
                        take(f"fg{hf}.{c}", f_g[:, c], 1.0, left)
                    root(2 + i)

                nu = TBH * FOX_H

                def probs(u):
                    keys = (TBH * hf + u // FOX_H + 1) * P
                    catch_up(position[f"sc{hf}.{u}"])
                    act.wait_ge(sem["negmax_ready"], nu * hf + u + 1)
                    if u >= 2:
                        full(act, f"pt{hf}.{u - 2}")
                    act.activation(f_p[:, u % 2, 0:keys], bank_of(f"sc{hf}.{u}")[:, 0:keys], ACT.Exp,
                                   bias=f_nm[:, u % 2:u % 2 + 1], accum_out=f_sum[:, u % 2:u % 2 + 1])\
                       .then_inc(sem["p_ready"], 1)

                probs(0)
                for u in range(nu):
                    keys = (TBH * hf + u // FOX_H + 1) * P
                    if u + 1 < nu:
                        probs(u + 1)
                    if u >= 2:
                        catch_up(position[f"pt{hf}.{u}"])
                        act.wait_ge(sem["mixed"], nu * hf + u - 1)
                    take(f"pt{hf}.{u}", f_pt[:, u % 2, 0:keys], 1.0, lambda b: b[:, 0:keys])
                    if u and (u - 1) % 8 == 7:
                        heads(hf, u - 1)
                heads(hf, nu - 1)
                act.wait_ge(sem["mixed"], nu * (hf + 1))
                act.activation(f_e, f_g, ACT.Exp, scale=-1.0).then_inc(sem["fsig_exp"], 1)

            def heads(hf, u):
                tb, half = u // FOX_H, u % FOX_H // 8
                catch_up(position[f"mix{hf}.{u}"])
                act.wait_ge(sem["mixed"], TBH * FOX_H * hf + u + 1)
                freed(act.activation(f_o[:, 4 * half:4 * half + 4, tb * P:(tb + 1) * P], four(banks[3][:]), ACT.Copy),
                      f"fo{hf}.{tb}.{half}")

            for q, stages in PLAN:
                open_window(q)
                if q is not None and not stages:
                    gather(q)
                for key in stages:
                    {"gla": gla, "route": route, "fox": fox}[key[0]](key)
                    if key[0] == "route":
                        catch_up(window[1])

        @block.gpsimd
        def _(pool):
            fetched = [0]

            def catch_up(x):
                while fetched[0] < min(x + 3, window[1]):
                    s = fetched[0]
                    fetched[0] += 1
                    b = s // BLOCK_STEPS
                    if s % BLOCK_STEPS == 0:
                        pool.wait_ge(sem["route_ready"], b + 1)
                    at = PAIR * s - b * NSEL + b % TBH * NSEL
                    r = PAIR * s % NSLOT
                    pool.wait_ge(sem["slots_used"], PAIR * s + PAIR)
                    for i in range(PAIR):
                        pool.indirect_dma_start(ring[:, r + i], None, uv,
                                                bass.IndirectOffsetOnAxis(ap=idx[:, b // TBH % 2, at + i:at + i + 1], axis=0))\
                            .then_inc(row_ready[r + i], 16)

            keep_up[pool.engine] = catch_up
            open_window(None)

            def gla(key):
                g = key[2]
                taken(pool, f"k{g}.3")
                e3 = g_e.rearrange("p (a b) -> p a b", a=GLA_H)
                for lev in range(8):
                    if lev:
                        i = 2 * lev - 1 if lev < 7 else 15
                        catch_up(position[f"g{g}.{i}" if i < DC else f"v{g}.{i - DC}"])
                    if lev < 7:
                        pool.wait_ge(sem["level_exp"], 7 * g + lev + 1)
                    else:
                        pool.wait_ge(sem["last_exp"], g + 1)
                    if lev:
                        full(pool, f"lev{g}.{lev - 1}.{TBH - 1}")
                    pool.tensor_tensor(g_kl, g_k, e3, ALU.mult).then_inc(sem["kl_ready"], 1)

            def gather(q):
                for tb in range(TBH):
                    b = TBH * q + tb
                    pool.wait_ge(sem["route_ready"], b + 1)
                    with pool.Fori(0, NSEL // NSLOT) as i:
                        for pr in range(NSLOT // PAIR):
                            r = PAIR * pr
                            pool.wait_ge(sem["slots_used"], i * NSLOT + (b * NSEL + r + PAIR))
                            pool.nop(nofuse=True)
                            pool.tensor_copy(idx_now[:, r:r + PAIR], idx[:, q % 2, bass.ds(i * NSLOT + (tb * NSEL + r), PAIR)])\
                                .then_inc(sem["idx_staged"], 1)
                            pool.wait_ge(sem["idx_staged"], i * (NSLOT // PAIR) + (tb * NSEL // PAIR + pr + 1))
                            pool.nop(nofuse=True)
                            for s in range(r, r + PAIR):
                                pool.indirect_dma_start(ring[:, s], None, uv,
                                                        bass.IndirectOffsetOnAxis(ap=idx_now[:, s:s + 1], axis=0))\
                                    .then_inc(row_ready[s], 16)

            for q, stages in PLAN:
                open_window(q)
                if q is not None and not stages:
                    gather(q)
                for key in stages:
                    if key[0] == "gla":
                        gla(key)
                    if key[0] == "route":
                        catch_up(window[1])


def layout(inputs):
    import numpy as np

    a = {k: np.asarray(v) for k, v in inputs.items()}

    def tiles(w):
        return w.reshape(DC, P, -1, P).transpose(2, 1, 0, 3)

    def small(w):
        return w.reshape(DC, P, -1).transpose(1, 0, 2)

    def column(v):
        return v.reshape(-1, P).T

    gla_in = a["gla_w_in"][0]
    kvf = a["fox_w_kvf"]
    wide = GLA_IN_WIDE
    keys = a["peer_sub_keys"].reshape(2, HP, NK, P)
    wt = np.empty((NTILES, P, DC, P), np.float32)
    for name, part in (("mod0", tiles(a["mod_w"][0])), ("mod1", tiles(a["mod_w"][1])), ("kvmod", tiles(a["kv_mod_w"])),
                       ("gla_in", tiles(gla_in[:, :wide])), ("gla_out", tiles(a["gla_w_out"][0])),
                       ("pq0", tiles(a["peer_w_q"][0])), ("pq1", tiles(a["peer_w_q"][1])),
                       ("keys0", keys[0].reshape(2, 8, NK, P).transpose(0, 3, 1, 2)),
                       ("keys1", keys[1].reshape(2, 8, NK, P).transpose(0, 3, 1, 2)),
                       ("fox_kv", tiles(kvf[:, :2 * D])), ("fox_qg", tiles(a["fox_w_qg"][0])),
                       ("fox_out", tiles(a["fox_w_out"][0]))):
        wt[TILES[name]:TILES[name] + len(part)] = part
    uv = np.empty((2 * EXPERTS, 2 * D), np.float32)
    uv[:, :D] = a["peer_u"].reshape(-1, D)
    uv[:, D:] = a["peer_v"].reshape(-1, D)
    col = np.zeros((P, NCOL), np.float32)
    col[:, COL_C:COL_C + DC] = column(a["c"][0])
    col[:, COL_MODB:COL_MODB + 96] = column(a["mod_b"].reshape(-1))
    col[:, COL_MODB + 96:COL_MODB + NMOD] = column(a["kv_mod_b"])
    col[:, COL_BG:COL_BG + GLA_H] = column(a["gla_b_gate"][0])
    col[:, COL_ON:COL_ON + 2] = column(a["gla_o_norm"][0])
    for half in range(2):
        col[half * FOX_HD:(half + 1) * FOX_HD, COL_KN] = a["fox_k_norm"]
        col[half * FOX_HD:(half + 1) * FOX_HD, COL_QN] = a["fox_q_norm"][0]
    col[:FOX_H, COL_BF] = a["fox_b_f"]
    wsmall = np.stack([small(gla_in[:, wide:]), small(kvf[:, 2 * D:])], axis=1).reshape(P, -1)
    const = np.zeros((P, NCONST), np.float32)
    at = np.arange(P)
    row, colm = at[:, None], at[None, :]
    const[:, K_ID:K_ID + P] = row == colm
    const[:, K_ONE:K_ONE + P] = 1
    const[:, K_BD:K_BD + P] = row // FOX_HD == colm // FOX_HD
    const[:, K_NEG:K_NEG + P] = np.where(colm > row, -1e30, 0)
    mask = np.empty((P, 8, P), np.float32)
    for lev, half in enumerate(LEVELS + [0]):
        m = row == colm if not half else ((row // (2 * half) == colm // (2 * half))
                                          & (row % (2 * half) < half) & (colm % (2 * half) >= half))
        mask[:, lev] = m
    const[:, K_IOTA:K_IOTA + TOPK] = np.arange(TOPK)
    return {"xt": a["x"][0].T, "wt": wt, "uv": uv, "cols": col, "consts": const, "masks": mask.reshape(P, -1), "small": wsmall,
            "wgate": a["gla_w_gate2"][0]}


GLA_IN_WIDE = 2 * GLA_H * GLA_HK + 2 * GLA_H * GLA_HV


def kernel(**inputs):
    import numpy as np
    import concourse.bacc as bacc
    from concourse.bass_utils import run_bass_kernel_spmd

    arrays = {n: np.ascontiguousarray(v) for n, v in layout(inputs).items()}
    nc = bacc.Bacc("TRN2", target_bir_lowering=False, num_devices=1)
    args = [nc.dram_tensor(f"in_{n}", a.shape, mybir.dt.from_np(a.dtype), kind="ExternalInput").ap()
            for n, a in arrays.items()]
    args.append(nc.dram_tensor("out_xt", (D, SEQ), F32, kind="ExternalOutput").ap())
    build(nc, *args)
    r = run_bass_kernel_spmd(nc, [{f"in_{n}": v for n, v in arrays.items()}], core_ids=[0])
    return np.ascontiguousarray(r.results[0]["out_xt"].T)[None]
```

```python
from contextlib import ExitStack

import concourse.bass as bass
from concourse import mybir

F32 = mybir.dt.float32
U32 = mybir.dt.uint32
U8 = mybir.dt.uint8
ALU = mybir.AluOpType
ACT = mybir.ActivationFunctionType
AX_X = mybir.AxisListType.X

P = 128
D = 1024
SEQ = 512
DC = D // P
HALF = 256
NHALF = SEQ // HALF
TBH = HALF // P
EPS = 1e-6
GLA_H, GLA_HK, GLA_HV, RANK = 4, 128, 256, 16
FOX_H, FOX_HD = 16, 64
PH, NK, TOPK = 8, 128, 16
EXPERTS = NK * NK
HP = 2 * PH
NSEL = PH * TOPK
LEVELS = [64, 32, 16, 8, 4, 2, 1]
NEG = -3.0e38

TILES = {}
_n = 0
for _name, _count in (("mod0", 48), ("mod1", 48), ("kvmod", 16), ("gla_in", 24), ("gla_out", 8),
                      ("pq0", 16), ("pq1", 16), ("keys0", 2), ("keys1", 2), ("fox_kv", 16),
                      ("fox_qg", 16), ("fox_out", 8)):
    TILES[_name] = _n
    _n += _count
NTILES = _n
WR = 4
MR = 8

COL_C = 0
COL_MODB = COL_C + DC
NMOD = 112
COL_BG = COL_MODB + NMOD
COL_ON = COL_BG + GLA_H
COL_KN = COL_ON + 2
COL_QN = COL_KN + 1
COL_BF = COL_QN + 1
NCOL = COL_BF + 1
K_ID, K_ONE, K_BD, K_NEG, K_ZERO, K_IOTA = 0, 128, 256, 384, 512, 640
NCONST = K_IOTA + 16

NSLOT = 8
PAIR = 2

SEMS = """x_loaded mask_loaded mixed const_loaded col_loaded small_loaded tile_started cpad_ready mod_tiles
 mods_ready sq_ready ms_ready rms_ready xn_ready h_ready hk_ready gate_abs gate_soft level_gap
 level_exp ql_ready kl_ready attn_ready last_gap last_exp chunk_exp state_ready sqo_ready mso_ready
 rmso_ready silu_exp silu_done o_ready s_free top_ready top_exp route_ready slots_used dot_ready
 gelu_ready diag_ready idx_staged loop_sums otok_ready dots_done fgate_abs fgate_soft cum_ready
 fsq_ready fms_ready frms_ready fn_ready negmax_ready p_ready pn_ready fsig_exp fgated act_chain
 dve_chain out_written""".split()


def build(nc, xt, wt, uv, cols, consts, masks, small, wgate, out):
    ctx = ExitStack()
    with ctx:
        def sb(name, shape, dt=F32):
            return ctx.enter_context(nc.sbuf_tensor(name, shape, dt))

        xT = sb("xT", [P, DC, SEQ])
        hT = sb("hT", [P, DC, HALF])
        wring = sb("wring", [P, WR, DC, P])
        const = sb("const", [P, NCONST])
        col = sb("col", [P, NCOL])
        levmask = sb("levmask", [P, 8, P], U8)
        wsmall = sb("wsmall", [P, 2, DC, 16])
        wg2 = sb("wg2", [RANK, GLA_H * GLA_HK])
        cpad = sb("cpad", [P, DC, 2 * MR - 1])
        mod = sb("mod", [P, NMOD])
        mod1 = sb("mod1", [P, NMOD])
        rms = sb("rms", [P, HALF])
        qn8 = sb("qn8", [P, 1])
        ring = sb("ring", [P, NSLOT, 2 * D])
        diag = sb("diag", [P, NSLOT, P])
        dots = sb("dots", [P, NSLOT])
        acts = sb("acts", [P, NSLOT])
        idx_now = sb("idx_now", [P, NSLOT], U32)
        htok = sb("htok", [P, 2, TBH, D])
        idx = sb("idx", [P, 2, TBH * NSEL], U32)
        gate = sb("gate", [P, 2, TBH * NSEL])
        ncum = sb("ncum", [FOX_H, SEQ])
        kvmem = sb("kvmem", [P, 8192])
        tmp = sb("tmp", [P, 9216])

        def view(mem, at, *dims, dt=None):
            n = 1
            for d in dims:
                n *= d
            v = mem[:, at:at + n]
            if dt is not None:
                v = v.bitcast(dt)
            names = "abc"[:len(dims)]
            if len(dims) == 1:
                return v
            return v.rearrange(f"p ({' '.join(names)}) -> p {' '.join(names)}",
                               **{k: d for k, d in zip(names[1:], dims[1:])})

        g_q = view(tmp, 0, GLA_H, HALF)
        g_k = view(tmp, 1024, GLA_H, HALF)
        g_b = view(tmp, 2048, GLA_H * HALF)
        g_d = view(tmp, 3072, GLA_H * HALF)
        g_e = view(tmp, 4096, GLA_H * HALF)
        g_ql = view(tmp, 5120, GLA_H, HALF)
        g_kl = view(tmp, 6144, GLA_H, HALF)
        g_attn = view(tmp, 7168, TBH, GLA_H, P)
        g_kd = view(tmp, 8192, TBH, GLA_H, P)
        g_sq = view(tmp, 3072, DC, HALF)
        g_rs = view(tmp, 5120, GLA_H, HALF)
        g_low = kvmem[0:RANK, 7168:7168 + HALF]
        g_el = view(kvmem, 7168 + HALF, GLA_H * TBH)
        g_g = view(kvmem, 0, DC, HALF)
        g_sig = view(kvmem, 7440, 2, HALF)
        g_v = view(kvmem, 2048, TBH, D)
        g_o = view(kvmem, 4096, DC, HALF)
        g_state = view(kvmem, 6144, GLA_H, GLA_HV)
        r_q = view(tmp, 0, HP, HALF)
        r_s = view(tmp, 4096, HP, NK)
        r_hot = view(tmp, 4096, NSEL, TOPK)
        r_cand = view(tmp, 6144, PH, TOPK * TOPK)
        r_v = view(tmp, 8192, HP, TOPK)
        r_i = view(tmp, 8448, HP, TOPK, dt=U32)
        r_if = view(tmp, 8704, HP, TOPK)
        r_ts = view(tmp, 8960, PH, TOPK)
        r_tc = view(tmp, 9088, PH, TOPK, dt=U32)
        r_hu = view(tmp, 6144, NSEL, dt=U32)
        r_hf = view(tmp, 6272, NSEL)
        r_sel = view(tmp, 6400, 2, NSEL)
        r_sum = view(tmp, 6656, PH)
        r_max = view(tmp, 6664, PH)
        f_hk = view(tmp, 0, DC, HALF)
        f_o = f_hk
        f_q = view(tmp, 2048, DC, HALF)
        f_g = view(tmp, 4096, DC, HALF)
        f_p = view(tmp, 6144, 2, SEQ)
        f_pt = view(tmp, 7168, 2, SEQ)
        f_sq = view(tmp, 6144, 4, HALF)
        f_rs = view(tmp, 7168, 4, HALF)
        f_z = tmp[0:FOX_H, 8192:8192 + HALF]
        f_a = tmp[0:FOX_H, 8448:8448 + HALF]
        f_k = view(kvmem, 0, DC, SEQ)
        f_v = view(kvmem, 4096, SEQ // P, D)
        f_nm = sb("f_nm", [P, 2])
        f_sum = sb("f_sum", [P, 2])
        f_inv = sb("f_inv", [P, 2])

        acc = ctx.enter_context(nc.psum_tensor("acc", [P, 2, 512], F32))
        banks = [ctx.enter_context(nc.psum_tensor(f"bank{i}", [P, 512], F32)) for i in range(6)]

        sem = {n: ctx.enter_context(nc.semaphore(n)) for n in SEMS}
        w_ready = [ctx.enter_context(nc.semaphore(f"w_ready{i}")) for i in range(WR)]
        row_ready = [ctx.enter_context(nc.semaphore(f"row_ready{i}")) for i in range(NSLOT)]
        x_mix = [[ctx.enter_context(nc.semaphore(f"x_mix{l}{h}")) for h in range(2)] for l in range(2)]
        x_ffn = [[ctx.enter_context(nc.semaphore(f"x_ffn{l}{h}")) for h in range(2)] for l in range(2)]
        bank_full = [ctx.enter_context(nc.semaphore(f"bank_full{i}")) for i in range(6)]
        bank_taken = [ctx.enter_context(nc.semaphore(f"bank_taken{i}")) for i in range(6)]

        mod_rows = [kvmem[0:MR, 0:256], tmp[0:MR, 8192:8192 + 384], kvmem[0:MR, 0:1152]]
        ident, ones, blockdiag = const[:, K_ID:K_ID + P], const[:, K_ONE:K_ONE + P], const[:, K_BD:K_BD + P]
        negmask = const[:, K_NEG:K_NEG + P]
        zeros = const[:, K_ZERO:K_ZERO + P]
        iota = const[:, K_IOTA:K_IOTA + TOPK]

        PLAN = [(None, [("gla", 0, 0), ("route", 0, 0)]),
                (0, [("gla", 0, 1), ("route", 0, 1)]),
                (1, [("fox", 1, 0), ("route", 1, 0)]),
                (2, [("fox", 1, 1), ("route", 1, 1)]),
                (3, [])]
        ORDER = [key for _, stages in PLAN for key in stages]
        LN = {s: n for n, s in enumerate(ORDER)}
        RT = {s[1:]: n for n, s in enumerate([s for s in ORDER if s[0] == "route"])}
        GATHER = {n: key for key, n in RT.items()}

        fills = {}
        nfill, nfull = [0] * 6, [0] * 6
        order_of_tiles = []

        BLOCK_STEPS = NSEL // PAIR
        HALF_STEPS = TBH * BLOCK_STEPS
        position = {}
        window = [0, 0]

        def full(eng, name):
            keep_up[eng.engine](position[name])
            b, _, n = fills[name]
            eng.wait_ge(bank_full[b], n)

        def taken(eng, name):
            keep_up[eng.engine](position[name])
            b, n, _ = fills[name]
            eng.wait_ge(bank_taken[b], n)

        keep_up = {}

        def bank_of(name):
            return banks[fills[name][0]]

        def freed(ins, name):
            ins.then_inc(bank_taken[fills[name][0]], 1)

        def open_window(q):
            window[1] = 0 if q is None else min(q + 1, len(GATHER) - 1) * HALF_STEPS

        def open_block():
            window[1] = BLOCK_STEPS

        def end_of_window(q):
            end = window[1] if q is not None else 0
            open_window(0 if q is None else q + 1)
            return end

        block = ctx.enter_context(nc.Block())

        @block.tensor
        def _(pe):
            keep_up[pe.engine] = lambda x: None
            open_window(None)
            begun = [0]
            credit = [0.0]

            def step(s):
                b = s // BLOCK_STEPS
                if b and s % BLOCK_STEPS == 0:
                    sums_copied(b - 1)
                for k in range(PAIR * s, PAIR * s + PAIR):
                    pe.wait_ge(sem["diag_ready"], k + 1)
                    sum_rows(k % NSLOT, k % NSEL == 0, k % NSEL == NSEL - 1)
                begun[0] = s + 1
                if (s + 1) % BLOCK_STEPS == 0:
                    turn_sums(b)

            def sum_rows(r, first=False, last=False):
                for c in range(2):
                    mm = pe.matmul(acc[:, c], diag[:, r], ring[:, r, D + 512 * c:D + 512 * (c + 1)],
                                   start=first, stop=last)
                mm.then_inc(sem["slots_used"], 1)

            def sums_copied(b):
                pe.wait_ge(sem["otok_ready"], b + 1)

            def turn_sums(b):
                sums_copied(b)
                for half in range(2):
                    turned = bank(f"sum{b}.{half}", 4 + half)
                    for i in range(4):
                        c = 4 * half + i
                        mm = pe.transpose(turned[:, i * P:(i + 1) * P],
                                          htok[:, b // TBH % 2, b % TBH, c * P:(c + 1) * P], ident)
                    done(mm, f"sum{b}.{half}")

            def weave(us):
                credit[0] += us
                while credit[0] >= pace[0]:
                    credit[0] -= pace[0]
                    if begun[0] < window[1]:
                        step(begun[0])

            def fill_gap(steps):
                for _ in range(steps):
                    if begun[0] < window[1]:
                        step(begun[0])

            pace = [3.0]

            def bank(name, b):
                if nfill[b]:
                    pe.wait_ge(bank_taken[b], nfill[b])
                nfill[b] += 1
                fills[name] = (b, nfill[b], None)
                position[name] = begun[0]
                return banks[b]

            def done(mm, name):
                b, n, _ = fills[name]
                nfull[b] += 1
                fills[name] = (b, n, nfull[b])
                position[name] = begun[0]
                mm.then_inc(bank_full[b], 1)

            def tile(which):
                j = len(order_of_tiles)
                order_of_tiles.append(which)
                pe.wait_ge(w_ready[j % WR], 16 * (j // WR + 1))
                return wring[:, j % WR], j

            def project(which, name, src, token_major=False):
                weave(3.5)
                w, j = tile(which)
                b = bank(name, 4 + j % 2)
                if not token_major:
                    for c in range(DC):
                        mm = pe.matmul(b[:, 0:HALF], w[:, c], src[:, c], start=c == 0, stop=c == DC - 1)
                        if c == 0:
                            mm.then_inc(sem["tile_started"], 1)
                else:
                    for tb in range(TBH):
                        for c in range(DC):
                            mm = pe.matmul(b[:, tb * P:(tb + 1) * P], src[:, c, tb * P:(tb + 1) * P], w[:, c],
                                           start=c == 0, stop=c == DC - 1)
                            if c == 0 and tb == 0:
                                mm.then_inc(sem["tile_started"], 1)
                done(mm, name)

            def mods(name, b, first, count, at=0):
                if not at:
                    bank(name, b)
                j0 = len(order_of_tiles)
                order_of_tiles.extend(range(first, first + count))
                with pe.Fori(0, count // MR) as i:
                    for r in range(MR):
                        slot = (j0 + r) % WR
                        pe.wait_ge(w_ready[slot], i * (16 * MR // WR) + 16 * ((j0 + r) // WR + 1))
                        pe.nop(nofuse=True)
                        for c in range(DC):
                            mm = pe.matmul(banks[b][0:MR, bass.ds(i * P + at, P)], cpad[:, c, MR - 1 - r:2 * MR - 1 - r],
                                           wring[:, slot, c], start=r == 0 and c == 0,
                                           stop=r == MR - 1 and c == DC - 1)
                            if c == 0:
                                mm.then_inc(sem["tile_started"], 1)
                        mm.then_inc(sem["mod_tiles"], 1)
                position[name] = begun[0]

            def mod_columns(n, count, parts=("",)):
                for part in parts:
                    taken(pe, f"mod.{n}{part}")
                b = bank(f"modT.{n}", 3)
                for g in range(count // MR):
                    mm = pe.transpose(b[:, g * MR:(g + 1) * MR], mod_rows[n][:, g * P:(g + 1) * P], ident[0:MR, 0:MR])
                done(mm, f"modT.{n}")

            def adaln(key):
                n = LN[key]
                fill_gap(2)
                pe.wait_ge(sem["sq_ready"], n + 1)
                b = bank(f"ms{n}", 0)
                for c in range(DC):
                    mm = pe.matmul(b[:, 0:HALF], ones, hT[:, c], start=c == 0, stop=c == DC - 1)
                done(mm, f"ms{n}")
                if key == ("gla", 0, 1):
                    mod_columns(2, 72, ("a", "b", "c"))
                fill_gap(2)
                return DC * n

            def gla(key):
                g = key[2]
                before = adaln(key)
                if g == 0:
                    pe.wait_ge(sem["small_loaded"], 32)
                b = bank(f"glow{g}", 0)
                for c in range(DC):
                    pe.wait_ge(sem["h_ready"], before + c + 1)
                    mm = pe.matmul(b[0:RANK, 0:HALF], wsmall[:, 0, c], hT[:, c], start=c == 0, stop=c == DC - 1)
                done(mm, f"glow{g}")
                t0 = TILES["gla_in"]
                project(t0, f"q{g}.0", hT)
                taken(pe, f"glow{g}")
                for i in range(2):
                    b = bank(f"gate{g}.{i}", 1 + i)
                    for h in (2 * i, 2 * i + 1):
                        mm = pe.matmul(b[:, (h % 2) * HALF:(h % 2 + 1) * HALF], wg2[:, h * P:(h + 1) * P],
                                       g_low, start=True, stop=True)
                    done(mm, f"gate{g}.{i}")
                for h in range(1, GLA_H):
                    project(t0 + h, f"q{g}.{h}", hT)
                for h in range(GLA_H):
                    project(t0 + 4 + h, f"k{g}.{h}", hT)
                rest = [(t0 + 16 + c, f"g{g}.{c}", False) for c in range(DC)]
                rest += [(t0 + 8 + c, f"v{g}.{c}", True) for c in range(DC)]
                for lev in range(8):
                    for w, name, tm in rest[2 * lev:2 * lev + 2]:
                        project(w, name, hT, tm)
                    if lev < 7:
                        pe.wait_ge(sem["ql_ready"], 8 * g + lev + 1)
                        pe.wait_ge(sem["kl_ready"], 8 * g + lev + 1)
                        ql, kl = g_ql, g_kl
                    else:
                        taken(pe, f"k{g}.3")
                        ql, kl = g_q, g_k
                    for tb in range(TBH):
                        ts = slice(tb * P, (tb + 1) * P)
                        b = bank(f"lev{g}.{lev}.{tb}", tb)
                        for h in range(GLA_H):
                            mm = pe.matmul(b[:, h * P:(h + 1) * P], kl[:, h, ts], ql[:, h, ts], start=True, stop=True)
                        done(mm, f"lev{g}.{lev}.{tb}")
                    weave(1.8)
                pe.wait_ge(sem["kl_ready"], 8 * (g + 1))
                for tb in range(TBH):
                    b = bank(f"kd{g}.{tb}", tb)
                    for h in range(GLA_H):
                        mm = pe.transpose(b[:, h * P:(h + 1) * P], g_kl[:, h, tb * P:(tb + 1) * P], ident)
                    done(mm, f"kd{g}.{tb}")
                pe.wait_ge(sem["attn_ready"], g + 1)
                taken(pe, f"v{g}.7")
                pe.wait_ge(sem["ql_ready"], 8 * (g + 1))
                for tb in range(TBH):
                    block_no = TBH * g + tb
                    ts = slice(tb * P, (tb + 1) * P)
                    if block_no:
                        pe.wait_ge(sem["state_ready"], block_no)
                    for half in range(2):
                        name = f"o{g}.{tb}.{half}"
                        b = bank(name, 2 + half)
                        for i in range(4):
                            h, vc = (4 * half + i) // 2, (4 * half + i) % 2
                            o = b[:, i * P:(i + 1) * P]
                            mm = pe.matmul(o, g_v[:, tb, (4 * half + i) * P:(4 * half + i + 1) * P],
                                           g_attn[:, tb, h], start=True, stop=block_no == 0)
                            if block_no:
                                mm = pe.matmul(o, g_state[:, h, vc * P:(vc + 1) * P], g_ql[:, h, ts],
                                               start=False, stop=True)
                        done(mm, name)
                    if block_no < NHALF * TBH - 1:
                        taken(pe, f"kd{g}.{tb}")
                        for half in range(2):
                            name = f"st{g}.{tb}.{half}"
                            b = bank(name, half)
                            for h in (2 * half, 2 * half + 1):
                                mm = pe.matmul(b[:, (h % 2) * GLA_HV:(h % 2 + 1) * GLA_HV], g_kd[:, tb, h],
                                               g_v[:, tb, h * GLA_HV:(h + 1) * GLA_HV], start=True, stop=True)
                            done(mm, name)
                if g == 0:
                    mods("mod.1", 3, 16, 16)
                fill_gap(1)
                pe.wait_ge(sem["sqo_ready"], g + 1)
                for half in range(2):
                    name = f"mso{g}.{half}"
                    b = bank(name, half)
                    for h in (2 * half, 2 * half + 1):
                        for vc in range(2):
                            mm = pe.matmul(b[:, (h % 2) * HALF:(h % 2 + 1) * HALF], ones, g_sq[:, 2 * h + vc],
                                           start=vc == 0, stop=vc == 1)
                    done(mm, name)
                if g == 0:
                    mods("mod.1", 3, 32, MR, 2 * P)
                    mod_columns(1, 24)
                fill_gap(3)
                pe.wait_ge(sem["o_ready"], 2 * (g + 1))
                for c in range(DC):
                    project(TILES["gla_out"] + c, f"mix0{g}.{c}", g_o)

            def route(key):
                l, hf = key[1:]
                r = RT[l, hf]
                before = adaln(key)
                for b4 in range(4):
                    name = f"htok{r}.{b4}"
                    b = bank(name, b4)
                    tb, half = b4 // 2, b4 % 2
                    for i in range(4):
                        pe.wait_ge(sem["h_ready"], before + half * 4 + i + 1)
                        mm = pe.transpose(b[:, i * P:(i + 1) * P], hT[:, half * 4 + i, tb * P:(tb + 1) * P], ident)
                    done(mm, name)
                for j in range(HP):
                    project(TILES[f"pq{l}"] + j, f"pq{r}.{j}", hT)
                fill_gap(1)
                taken(pe, f"pq{r}.{HP - 1}")
                for tb in range(TBH):
                    for kt in range(2):
                        w, _ = tile(TILES[f"keys{l}"] + kt)
                        for half in range(2):
                            name = f"s{r}.{tb}.{2 * kt + half}"
                            b = bank(name, 2 * kt + half)
                            for i in range(4):
                                mm = pe.matmul(b[:, i * P:(i + 1) * P],
                                               r_q[:, kt * 8 + half * 4 + i, tb * P:(tb + 1) * P],
                                               w[:, half * 4 + i], start=True, stop=True)
                                if half == 0 and i == 0:
                                    mm.then_inc(sem["tile_started"], 1)
                            done(mm, name)
                if r == 0:
                    open_block()
                    mods("mod.2a", 4, 40, MR)
                    for n in range(8):
                        mods("mod.2b" if n < 4 else "mod.2c", 4 + n // 4, 48 + MR * n, MR, n % 4 * P)
                        if n >= 2:
                            fill_gap(3)

            def gather(q):
                for b in range(TBH * q, TBH * q + TBH):
                    sums_copied(b - 1)
                    for c in range(2):
                        pe.matmul(acc[:, c], zeros, const[:, 0:512], start=True, stop=False)
                    with pe.Fori(0, NSEL // NSLOT) as i:
                        for r in range(NSLOT):
                            pe.wait_ge(sem["diag_ready"], i * NSLOT + (b * NSEL + r + 1))
                            sum_rows(r)
                    for c in range(2):
                        mm = pe.matmul(acc[:, c], zeros, const[:, 0:512], start=False, stop=True)
                    mm.then_inc(sem["loop_sums"], 1)
                    turn_sums(b)

            def fox(key):
                hf = key[2]
                before = adaln(key)
                b = bank(f"f{hf}", 1)
                for c in range(DC):
                    pe.wait_ge(sem["hk_ready"], DC * hf + c + 1)
                    mm = pe.matmul(b[0:FOX_H, 0:HALF], wsmall[:, 1, c], f_hk[:, c], start=c == 0, stop=c == DC - 1)
                done(mm, f"f{hf}")

                def norm(what, i, sq_no):
                    pe.wait_ge(sem["fsq_ready"], 4 * hf + sq_no + 1)
                    for half in range(2):
                        name = f"fms{hf}.{what}{i}.{half}"
                        b = bank(name, 2 + half)
                        for m in range(2):
                            mm = pe.matmul(b[:, m * HALF:(m + 1) * HALF], blockdiag, f_sq[:, 2 * half + m],
                                           start=True, stop=True)
                        done(mm, name)

                for c in range(DC):
                    project(TILES["fox_kv"] + c, f"fk{hf}.{c}", f_hk)
                for c in range(DC):
                    project(TILES["fox_kv"] + DC + c, f"fv{hf}.{c}", f_hk, True)
                    if c in (3, 7):
                        norm("k", c // 4, c // 4)
                pe.wait_ge(sem["h_ready"], before + DC)
                for c in range(DC):
                    project(TILES["fox_qg"] + c, f"fq{hf}.{c}", hT)
                for c in range(DC):
                    project(TILES["fox_qg"] + DC + c, f"fg{hf}.{c}", hT)
                    if c in (3, 7):
                        norm("q", c // 4, 2 + c // 4)
                fill_gap(2)
                pe.wait_ge(sem["fn_ready"], 4 * (hf + 1))
                pe.wait_ge(sem["cum_ready"], hf + 1)
                taken(pe, f"fv{hf}.{DC - 1}")

                units = [(tb, h) for tb in range(TBH) for h in range(FOX_H)]

                def scores(u):
                    tb, h = units[u]
                    keys = (TBH * hf + tb + 1) * P
                    pb, c, ts = FOX_HD * (h % 2), h // 2, slice(tb * P, (tb + 1) * P)
                    b = bank(f"sc{hf}.{u}", u % 2)
                    pe.matmul(b[:, 0:keys], f_q[pb:pb + FOX_HD, c, ts], f_k[pb:pb + FOX_HD, c, 0:keys],
                              start=True, stop=False)
                    pe.matmul(b[:, 0:keys], ident[0:FOX_H, h:h + 1].to_broadcast([FOX_H, P]), ncum[:, 0:keys],
                              start=False, stop=False)
                    mm = pe.matmul(b[:, keys - P:keys], ident, negmask, start=False, stop=True)
                    done(mm, f"sc{hf}.{u}")

                def turn(u):
                    tb, h = units[u]
                    pe.wait_ge(sem["pn_ready"], len(units) * hf + u + 1)
                    b = bank(f"pt{hf}.{u}", 2)
                    for kb in range(TBH * hf + tb + 1):
                        mm = pe.transpose(b[:, kb * P:(kb + 1) * P], f_p[:, u % 2, kb * P:(kb + 1) * P], ident)
                    done(mm, f"pt{hf}.{u}")

                def mix(u):
                    tb, h = units[u]
                    taken(pe, f"pt{hf}.{u}")
                    name = f"fo{hf}.{tb}.{h // 8}"
                    b = bank(name, 3) if h % 8 == 0 else banks[3]
                    pb, c = FOX_HD * (h % 2), (h // 2) % 4
                    for kb in range(TBH * hf + tb + 1):
                        mm = pe.matmul(b[pb:pb + FOX_HD, c * P:(c + 1) * P], f_v[:, kb, h * FOX_HD:(h + 1) * FOX_HD],
                                       f_pt[:, u % 2, kb * P:(kb + 1) * P], start=kb == 0,
                                       stop=kb == TBH * hf + tb)
                    mm.then_inc(sem["mixed"], 1)
                    position[f"mix{hf}.{u}"] = begun[0]

                scores(0)
                for u in range(len(units) + 1):
                    if u + 1 < len(units):
                        scores(u + 1)
                    weave(1.0)
                    if u < len(units):
                        turn(u)
                    weave(1.0)
                    if u:
                        mix(u - 1)
                    weave(0.9)
                fill_gap(1)
                pe.wait_ge(sem["fgated"], hf + 1)
                for c in range(DC):
                    project(TILES["fox_out"] + c, f"mix1{hf}.{c}", f_o)

            pe.wait_ge(sem["const_loaded"], 16)
            pe.wait_ge(sem["cpad_ready"], 1)
            mods("mod.0", 3, 0, 16)
            mod_columns(0, 16)
            for q, stages in PLAN:
                open_window(q)
                pace[0] = {0: 3.0, 1: 3.6, 2: 3.6}.get(q, 3.0)
                if q is not None and not stages:
                    gather(q)
                for key in stages:
                    {"gla": gla, "route": route, "fox": fox}[key[0]](key)
                    if key[0] == "route":
                        end = end_of_window(q)
                        while begun[0] < end:
                            step(begun[0])

        @block.sync
        def _(sp):
            keep_up[sp.engine] = lambda x: None
            open_window(None)
            sp.dma_start(col[:], cols).then_inc(sem["col_loaded"], 16)
            for j in range(WR):
                sp.dma_start(wring[:, j], wt[order_of_tiles[j]]).then_inc(w_ready[j], 16)
            sp.dma_start(const[:], consts).then_inc(sem["const_loaded"], 16)
            sp.dma_start(xT[:], xt.rearrange("(c p) t -> p c t", p=P)).then_inc(sem["x_loaded"], 16)
            sp.dma_start(view(tmp, 7168, 8 * P), masks).then_inc(sem["mask_loaded"], 16)
            sp.dma_start(wsmall[:].rearrange("p a c n -> p (a c n)"), small).then_inc(sem["small_loaded"], 16)
            sp.dma_start(wg2[:], wgate).then_inc(sem["small_loaded"], 16)
            at = WR
            while at < len(order_of_tiles):
                n = 1
                while at + n < len(order_of_tiles) and order_of_tiles[at + n] == order_of_tiles[at] + n:
                    n += 1
                first = order_of_tiles[at]
                if n < 2 * WR or at % WR:
                    head = n if n < 2 * WR else (-at) % WR
                    for j in range(at, at + head):
                        sp.wait_ge(sem["tile_started"], j - WR + 2)
                        sp.dma_start(wring[:, j % WR], wt[order_of_tiles[j]]).then_inc(w_ready[j % WR], 16)
                    at += head
                    continue
                with sp.Fori(0, n // WR) as i:
                    for r in range(WR):
                        sp.wait_ge(sem["tile_started"], i * WR + (at + r - WR + 2))
                        sp.dma_start(wring[:, r], wt[bass.ds(i * WR + (first + r), 1)].rearrange("o p c n -> (o p) c n"))\
                            .then_inc(w_ready[r], 16)
                at += n // WR * WR
            for hf in range(NHALF):
                sp.wait_ge(x_ffn[1][hf], DC * TBH)
                sp.dma_start(out.rearrange("(c p) t -> p c t", p=P)[:, :, hf * HALF:(hf + 1) * HALF],
                             xT[:, :, hf * HALF:(hf + 1) * HALF]).then_inc(sem["out_written"], 16)
            sp.wait_ge(sem["out_written"], 32)

        def half_of(hf):
            return slice(hf * HALF, (hf + 1) * HALF)

        @block.vector
        def _(dve):
            chain = [0]

            def mark(ins):
                chain[0] += 1
                ins.then_inc(sem["dve_chain"], 1)

            def settle():
                dve.wait_ge(sem["dve_chain"], chain[0])

            def link(ins):
                mark(ins)
                settle()

            def mod_batch(n, first, count):
                full(dve, f"modT.{n}")
                at = slice(first, first + count)
                link(dve.tensor_tensor(mod[:, at], banks[3][:, 0:count], col[:, COL_MODB + first:COL_MODB + first + count],
                                       ALU.add))
                link(dve.tensor_scalar(mod1[:, at], mod[:, at], 1.0, None, ALU.add))
                dve.sem_inc(bank_taken[3], 1)
                dve.sem_inc(sem["mods_ready"], 1)

            def adaln(key):
                kind, l, hf = key
                n = LN[key]
                full(dve, f"ms{n}")
                freed(dve.tensor_scalar(rms[:], bank_of(f"ms{n}")[:, 0:HALF], 1.0 / D, EPS, ALU.mult, ALU.add), f"ms{n}")
                taken(dve, f"ms{n}")
                dve.sem_inc(sem["ms_ready"], 1)
                dve.wait_ge(sem["rms_ready"], n + 1)
                link(dve.reciprocal(rms[:], rms[:]))
                for cs in (slice(0, DC // 2), slice(DC // 2, DC)):
                    dve.tensor_tensor(hT[:, cs], xT[:, cs, half_of(hf)],
                                      rms[:].rearrange("p (o t) -> p o t", o=1).to_broadcast([P, DC // 2, HALF]),
                                      ALU.mult).then_inc(sem["xn_ready"], 1)

            def add_residual(l, hf, names, gate_at, signal):
                for c in range(DC):
                    full(dve, names[c])
                    x = xT[:, c, half_of(hf)]
                    freed(dve.scalar_tensor_tensor(x, bank_of(names[c])[:, 0:HALF], mod[:, gate_at + c:gate_at + c + 1],
                                                   x, ALU.mult, ALU.add), names[c])
                dve.drain().then_inc(signal, DC)

            dotted, weighed, added, here, credit = [0], [0], [0], [0], [0.0]

            def begin(b):
                dve.wait_ge(sem["route_ready"], b + 1)
                htok_bank, n, _ = fills[f"htok{b // TBH}.3"]
                dve.wait_ge(bank_taken[htok_bank], n)

            def dot(r, q, tb):
                u = ring[:, r, 0:D]
                dve.tensor_tensor_reduce(u, u, htok[:, q % 2, tb], 1.0, 0.0, ALU.mult, ALU.add,
                                         dots[:, r:r + 1]).then_inc(sem["dot_ready"], 1)

            def weigh(r, gate_of):
                dve.tensor_scalar(diag[:, r], ident, acts[:, r:r + 1], gate_of, ALU.mult, ALU.mult)\
                   .then_inc(sem["diag_ready"], 1)

            def add_block(b):
                l, hf = GATHER[b // TBH]
                tb = b % TBH
                for half in range(2):
                    name = f"sum{b}.{half}"
                    full(dve, name)
                    for i in range(4):
                        c, at = 4 * half + i, hf * HALF + tb * P
                        x = xT[:, c, at:at + P]
                        ins = dve.scalar_tensor_tensor(x, bank_of(name)[:, i * P:(i + 1) * P],
                                                       mod[:, 48 * l + 40 + c:48 * l + 41 + c], x, ALU.mult, ALU.add)
                        if i < 3:
                            ins.then_inc(x_ffn[l][hf], 1)
                    freed(ins, name)
                taken(dve, f"sum{b}.0")
                taken(dve, f"sum{b}.1")
                dve.sem_inc(x_ffn[l][hf], 2)
                if tb == TBH - 1:
                    dve.sem_inc(sem["dots_done"], 1)

            def catch_up(x):
                for at in range(here[0], min(x, window[1]) + 1):
                    here[0] = at
                    keep_step(at)

            def keep_step(x):
                while dotted[0] < min(x + 2, window[1]) or weighed[0] < min(x + 1, window[1]):
                    s = dotted[0]
                    if s < min(x + 2, window[1]):
                        dotted[0] += 1
                        if s % BLOCK_STEPS == 0:
                            begin(s // BLOCK_STEPS)
                        b = s // BLOCK_STEPS
                        for k in range(PAIR * s, PAIR * s + PAIR):
                            r = k % NSLOT
                            dve.wait_ge(row_ready[r], 16 * (k // NSLOT + 1))
                            dot(r, b // TBH, b % TBH)
                    w = weighed[0]
                    if w < min(x + 1, window[1]) and (w < dotted[0] - 1 or dotted[0] == window[1]
                                                      or dotted[0] >= min(x + 2, window[1])):
                        weighed[0] += 1
                        b = w // BLOCK_STEPS
                        dve.wait_ge(sem["gelu_ready"], w + 1)
                        for k in range(PAIR * w, PAIR * w + PAIR):
                            at = k - b * NSEL + b % TBH * NSEL
                            weigh(k % NSLOT, gate[:, b // TBH % 2, at:at + 1])
                while added[0] < x // BLOCK_STEPS:
                    added[0] += 1
                    add_block(added[0] - 1)

            def work(us):
                credit[0] += us
                while credit[0] >= 2.6:
                    credit[0] -= 2.6
                    catch_up(here[0] + 1)

            def told(name, n):
                position[name, n] = here[0]

            keep_up[dve.engine] = catch_up
            open_window(None)

            def log_sigmoid_first(z, a, signal):
                dve.scalar_tensor_tensor(a, z, -1.0, z, ALU.mult, ALU.min).then_inc(signal, 1)

            def log_sigmoid_last(z, a):
                link(dve.scalar_tensor_tensor(z, z, 0.0, a, ALU.min, ALU.subtract))

            def gla(key):
                g = key[2]
                adaln(key)
                if g == 0:
                    dve.wait_ge(sem["mask_loaded"], 16)
                    link(dve.tensor_copy(levmask[:], view(tmp, 7168, 8, P)))
                else:
                    mod_batch(2, 40, 72)
                link(dve.memset(g_attn, 0.0))
                d3 = g_d.rearrange("p (a b) -> p a b", a=GLA_H)
                for i in range(2):
                    name = f"gate{g}.{i}"
                    full(dve, name)
                    b = bank_of(name)
                    for h in (2 * i, 2 * i + 1):
                        ins = dve.tensor_scalar(d3[:, h], b[:, (h % 2) * HALF:(h % 2 + 1) * HALF],
                                                col[:, COL_BG + h:COL_BG + h + 1], None, ALU.add)
                    freed(ins, name)
                    taken(dve, name)
                log_sigmoid_first(g_d, g_e, sem["gate_abs"])
                dve.wait_ge(sem["gate_soft"], g + 1)
                log_sigmoid_last(g_d, g_e)
                for i in range(GLA_H * TBH):
                    ts = slice(i * P, (i + 1) * P)
                    mark(dve.tensor_tensor_scan(g_b[:, ts], ones, g_d[:, ts], 0.0, ALU.mult, ALU.add))
                settle()

                def keep(lev):
                    for tb in range(TBH):
                        name = f"lev{g}.{lev}.{tb}"
                        full(dve, name)
                        m = levmask[:, lev].rearrange("p (o b) -> p o b", o=1).to_broadcast([P, GLA_H, P])
                        freed(dve.copy_predicated(g_attn[:, tb], m, bank_of(name)[:].rearrange("p (a b) -> p a b", a=GLA_H)),
                              name)

                def silu(pair):
                    dve.wait_ge(sem["silu_exp"], 4 * g + pair + 1)
                    two = g_g[:, 2 * pair:2 * pair + 2]
                    link(dve.tensor_scalar(g_sig, g_sig, 1.0, None, ALU.add))
                    link(dve.reciprocal(g_sig, g_sig))
                    dve.tensor_tensor(two, two, g_sig, ALU.mult).then_inc(sem["silu_done"], 1)

                for lev, half in enumerate(LEVELS):
                    nb = GLA_H * HALF // (2 * half)
                    bv = g_b.rearrange("p (n t) -> p n t", n=nb)
                    dv = g_d.rearrange("p (n t) -> p n t", n=nb)
                    link(dve.tensor_tensor(dv, bv, bv[:, :, half - 1:half].to_broadcast([P, nb, 2 * half]), ALU.subtract))
                    if lev:
                        dve.wait_ge(sem["kl_ready"], 8 * g + lev)
                    dve.scalar_tensor_tensor(g_e, g_d, -1.0, g_d, ALU.mult, ALU.min).then_inc(sem["level_gap"], 1)
                    if lev:
                        keep(lev - 1)
                    if lev == 0:
                        taken(dve, f"k{g}.3")
                    dve.wait_ge(sem["level_exp"], 7 * g + lev + 1)
                    dve.tensor_tensor(g_ql, g_q, g_e.rearrange("p (a b) -> p a b", a=GLA_H), ALU.mult)\
                       .then_inc(sem["ql_ready"], 1)
                    if lev >= 5:
                        silu(lev - 5)
                bv = g_b.rearrange("p (n t) -> p n t", n=GLA_H * TBH)
                dve.wait_ge(sem["kl_ready"], 8 * g + 7)
                dve.wait_ge(sem["ql_ready"], 8 * g + 7)
                dve.tensor_tensor(g_e.rearrange("p (n t) -> p n t", n=GLA_H * TBH),
                                  bv[:, :, P - 1:P].to_broadcast([P, GLA_H * TBH, P]), bv, ALU.subtract)\
                   .then_inc(sem["last_gap"], 1)
                keep(6)
                silu(2)
                keep(7)
                dve.drain().then_inc(sem["attn_ready"], 1)
                silu(3)
                dve.wait_ge(sem["chunk_exp"], g + 1)
                mark(dve.tensor_copy(g_el.rearrange("p (n o) -> p n o", o=1),
                                     g_d.rearrange("p (n t) -> p n t", n=GLA_H * TBH)[:, :, P - 1:P]))
                dve.tensor_tensor(g_ql, g_q, d3, ALU.mult).then_inc(sem["ql_ready"], 1)
                settle()
                for tb in range(TBH):
                    block_no = TBH * g + tb
                    if block_no == NHALF * TBH - 1:
                        break
                    for half in range(2):
                        name = f"st{g}.{tb}.{half}"
                        full(dve, name)
                        for h in (2 * half, 2 * half + 1):
                            new = bank_of(name)[:, (h % 2) * GLA_HV:(h % 2 + 1) * GLA_HV]
                            if block_no == 0:
                                ins = dve.tensor_copy(g_state[:, h], new)
                            else:
                                ins = dve.scalar_tensor_tensor(g_state[:, h], g_state[:, h],
                                                               g_el[:, h * TBH + tb:h * TBH + tb + 1], new,
                                                               ALU.mult, ALU.add)
                        freed(ins, name)
                    taken(dve, f"st{g}.{tb}.1")
                    dve.sem_inc(sem["state_ready"], 1)
                for half in range(2):
                    name = f"mso{g}.{half}"
                    full(dve, name)
                    freed(dve.tensor_scalar(g_rs[:, 2 * half:2 * half + 2], bank_of(name)[:].rearrange("p (a b) -> p a b", a=2),
                                            1.0 / GLA_HV, EPS, ALU.mult, ALU.add), name)
                dve.drain().then_inc(sem["mso_ready"], 1)
                catch_up(here[0] + 1)
                dve.wait_ge(sem["rmso_ready"], g + 1)
                link(dve.reciprocal(g_rs, g_rs))
                ov = g_o.rearrange("p (h v) t -> p h v t", h=GLA_H)
                sv = g_g.rearrange("p (h v) t -> p h v t", h=GLA_H)
                for vc in range(2):
                    mark(dve.tensor_tensor(ov[:, :, vc], ov[:, :, vc], g_rs, ALU.mult))
                settle()
                dve.wait_ge(sem["silu_done"], 4 * (g + 1))
                for vc in range(2):
                    dve.scalar_tensor_tensor(ov[:, :, vc], ov[:, :, vc], col[:, COL_ON + vc:COL_ON + vc + 1],
                                             sv[:, :, vc], ALU.mult, ALU.mult).then_inc(sem["o_ready"], 1)
                if g == 0:
                    mod_batch(1, 16, 24)
                add_residual(0, g, [f"mix0{g}.{c}" for c in range(DC)], 16, x_mix[0][g])

            def top16(values, indices, src):
                n = src.shape[1]
                us = 0.06 + src.shape[2] / 960.0
                for i in range(n):
                    mark(dve.max(values[:, i, 0:8], src[:, i]))
                    work(us)
                settle()
                for i in range(n):
                    mark(dve.max_index(indices[:, i, 0:8], values[:, i, 0:8], src[:, i]))
                    work(us)
                for i in range(n):
                    mark(dve.match_replace(src[:, i], values[:, i, 0:8], src[:, i], NEG))
                    work(us)
                settle()
                for i in range(n):
                    mark(dve.max(values[:, i, 8:16], src[:, i]))
                    work(us)
                settle()
                for i in range(n):
                    mark(dve.max_index(indices[:, i, 8:16], values[:, i, 8:16], src[:, i]))
                    work(us)
                settle()

            def route(key):
                l, hf = key[1:]
                r = RT[l, hf]
                adaln(key)
                for tb in range(TBH):
                    taken(dve, f"s{r}.{tb}.3")
                    top16(r_v, r_i, r_s)
                    mark(dve.tensor_copy(r_if, r_i))
                    halves = r_v.rearrange("p (h s) k -> p h s k", s=2)
                    link(dve.tensor_tensor(r_cand.rearrange("p h (a b) -> p h a b", a=TOPK),
                                           halves[:, :, 0].unsqueeze(3).to_broadcast([P, PH, TOPK, TOPK]),
                                           halves[:, :, 1].unsqueeze(2).to_broadcast([P, PH, TOPK, TOPK]), ALU.add))
                    top16(r_ts, r_tc, r_cand)
                    mark(dve.tensor_copy(r_max.unsqueeze(2), r_ts[:, :, 0:1]))
                    settle()
                    dve.tensor_tensor(r_ts, r_ts, r_max.unsqueeze(2).to_broadcast([P, PH, TOPK]), ALU.subtract)\
                       .then_inc(sem["top_ready"], 1)
                    told("top_ready", TBH * r + tb + 1)
                    for side in range(2):
                        tc = r_tc.rearrange("p a b -> p (a b)")
                        if side == 0:
                            link(dve.tensor_scalar(r_hu, tc, 4, None, ALU.logical_shift_right))
                        else:
                            link(dve.tensor_scalar(r_hu, tc, TOPK - 1, None, ALU.bitwise_and))
                        link(dve.tensor_copy(r_hf, r_hu))
                        link(dve.tensor_tensor(r_hot, r_hf.unsqueeze(2).to_broadcast([P, NSEL, TOPK]),
                                               iota.unsqueeze(1).to_broadcast([P, NSEL, TOPK]), ALU.is_equal))
                        hot = r_hot.rearrange("p (h k) a -> p h k a", h=PH)
                        names = r_if.rearrange("p (h s) k -> p h s k", s=2)[:, :, side]
                        link(dve.tensor_tensor(hot, hot, names.unsqueeze(2).to_broadcast([P, PH, TOPK, TOPK]), ALU.mult))
                        work(5.0)
                        mark(dve.tensor_reduce(r_sel[:, side], r_hot, AX_X, ALU.add))
                        work(2.3)
                    settle()
                    if r >= 2:
                        dve.wait_ge(sem["slots_used"], NSEL * TBH * (r - 1))
                    mine = slice(tb * NSEL, (tb + 1) * NSEL)
                    link(dve.scalar_tensor_tensor(r_hf, r_sel[:, 0], float(NK), r_sel[:, 1], ALU.mult, ALU.add))
                    mark(dve.tensor_scalar(idx[:, r % 2, mine], r_hf, float(l * EXPERTS), None, ALU.add))
                    dve.wait_ge(sem["top_exp"], TBH * r + tb + 1)
                    link(dve.tensor_reduce(r_sum, r_ts, AX_X, ALU.add))
                    link(dve.reciprocal(r_sum, r_sum))
                    dve.tensor_tensor(gate[:, r % 2, mine].rearrange("p (h k) -> p h k", h=PH), r_ts,
                                      r_sum.unsqueeze(2).to_broadcast([P, PH, TOPK]), ALU.mult)\
                       .then_inc(sem["route_ready"], 1)
                    dve.drain().then_inc(sem["s_free"], 1)
                    told("s_free", TBH * r + tb + 1)
                    if TBH * r + tb == 0:
                        open_block()

            def gather(q):
                for tb in range(TBH):
                    b = TBH * q + tb
                    begin(b)
                    with dve.Fori(0, NSEL // NSLOT) as i:
                        for pr in range(NSLOT // PAIR):
                            for r in range(PAIR * pr, PAIR * pr + PAIR):
                                dve.wait_ge(row_ready[r], i * 16 + 16 * (b * NSEL // NSLOT + 1))
                                dot(r, q, tb)
                            dve.wait_ge(sem["gelu_ready"], i * (NSLOT // PAIR) + (b * NSEL // PAIR + pr + 1))
                            for r in range(PAIR * pr, PAIR * pr + PAIR):
                                weigh(r, gate[:, q % 2, bass.ds(i * NSLOT + (tb * NSEL + r), 1)])
                    add_block(b)

            def fox(key):
                hf = key[2]
                if hf == 0:
                    link(dve.tensor_scalar(qn8[:], col[:, COL_QN:COL_QN + 1], FOX_HD ** -0.5, None, ALU.mult))
                adaln(key)
                name = f"f{hf}"
                full(dve, name)
                freed(dve.tensor_scalar(f_z, bank_of(name)[0:FOX_H, 0:HALF], col[0:FOX_H, COL_BF:COL_BF + 1], None,
                                        ALU.add), name)
                taken(dve, name)
                log_sigmoid_first(f_z, f_a, sem["fgate_abs"])
                dve.wait_ge(sem["fgate_soft"], hf + 1)
                link(dve.scalar_tensor_tensor(f_z, f_z, 0.0, f_a, ALU.min, ALU.subtract))
                at = hf * HALF
                one_row = ones[0:FOX_H, 0:1].to_broadcast([FOX_H, HALF])
                dve.tensor_tensor_scan(ncum[:, at:at + HALF], one_row, f_z,
                                       ncum[:, at - 1:at] if hf else 0.0, ALU.mult, ALU.subtract)\
                   .then_inc(sem["cum_ready"], 1)

                def norm(x, what, i, sq_no, gain):
                    if 4 * hf + sq_no:
                        dve.wait_ge(sem["fn_ready"], 4 * hf + sq_no)
                    for half in range(2):
                        name = f"fms{hf}.{what}{i}.{half}"
                        full(dve, name)
                        freed(dve.tensor_scalar(f_rs[:, 2 * half:2 * half + 2], bank_of(name)[:].rearrange("p (a b) -> p a b", a=2),
                                                1.0 / FOX_HD, EPS, ALU.mult, ALU.add), name)
                    dve.drain().then_inc(sem["fms_ready"], 1)
                    catch_up(position[(f"fv{hf}.5", f"fq{hf}.1", f"fg{hf}.5", f"fg{hf}.7")[sq_no]])
                    if sq_no == 3:
                        catch_up(here[0] + 1)
                    dve.wait_ge(sem["frms_ready"], 4 * hf + sq_no + 1)
                    link(dve.reciprocal(f_rs, f_rs))
                    dve.scalar_tensor_tensor(x, x, gain, f_rs, ALU.mult, ALU.mult).then_inc(sem["fn_ready"], 1)

                for i in range(2):
                    norm(f_k[:, 4 * i:4 * i + 4, half_of(hf)], "k", i, i, col[:, COL_KN:COL_KN + 1])
                for i in range(2):
                    norm(f_q[:, 4 * i:4 * i + 4], "q", i, 2 + i, qn8[:, 0:1])
                nu = TBH * FOX_H

                def negmax(u):
                    keys = (TBH * hf + u // FOX_H + 1) * P
                    name = f"sc{hf}.{u}"
                    full(dve, name)
                    dve.tensor_reduce(f_nm[:, u % 2:u % 2 + 1], bank_of(name)[:, 0:keys], AX_X, ALU.max, negate=True)\
                       .then_inc(sem["negmax_ready"], 1)

                def heads(u):
                    tb, half = u // FOX_H, u % FOX_H // 8
                    name = f"fo{hf}.{tb}.{half}"
                    catch_up(position[f"mix{hf}.{u}"])
                    dve.wait_ge(sem["mixed"], nu * hf + u + 1)
                    at = (slice(None), slice(4 * half, 4 * half + 4), slice(tb * P, (tb + 1) * P))
                    freed(dve.tensor_tensor(f_o[at], banks[3][:].rearrange("p (a b) -> p a b", a=4), f_g[at], ALU.mult), name)

                negmax(0)
                dve.wait_ge(sem["fsig_exp"], hf + 1)
                for u in range(nu):
                    keys = (TBH * hf + u // FOX_H + 1) * P
                    if u + 1 < nu:
                        negmax(u + 1)
                    dve.wait_ge(sem["p_ready"], nu * hf + u + 1)
                    at = slice(u % 2, u % 2 + 1)
                    freed(dve.reciprocal(f_inv[:, at], f_sum[:, at]), f"sc{hf}.{u}")
                    taken(dve, f"sc{hf}.{u}")
                    p = f_p[:, u % 2, 0:keys]
                    dve.tensor_scalar(p, p, f_inv[:, at], None, ALU.mult).then_inc(sem["pn_ready"], 1)
                    if u < DC:
                        link(dve.tensor_scalar(f_g[:, u], f_g[:, u], 1.0, None, ALU.add))
                        link(dve.reciprocal(f_g[:, u], f_g[:, u]))
                    if u > 2 and (u - 2) % 8 == 7:
                        heads(u - 2)
                heads(nu - 1)
                taken(dve, f"fo{hf}.{TBH - 1}.1")
                dve.sem_inc(sem["fgated"], 1)
                add_residual(1, hf, [f"mix1{hf}.{c}" for c in range(DC)], 64, x_mix[1][hf])

            dve.wait_ge(sem["col_loaded"], 16)
            link(dve.memset(cpad[:], 0.0))
            dve.tensor_copy(cpad[:, :, MR - 1:MR], col[:, COL_C:COL_C + DC].unsqueeze(2)).then_inc(sem["cpad_ready"], 1)
            dve.wait_ge(sem["const_loaded"], 16)
            mod_batch(0, 0, 16)
            for q, stages in PLAN:
                open_window(q)
                if q is not None and not stages:
                    gather(q)
                for key in stages:
                    {"gla": gla, "route": route, "fox": fox}[key[0]](key)
                    if key[0] == "route":
                        catch_up(end_of_window(q))

        @block.scalar
        def _(act):
            chain = [0]

            def link(ins):
                chain[0] += 1
                ins.then_inc(sem["act_chain"], 1)
                act.wait_ge(sem["act_chain"], chain[0])

            activated, summed, here = [0], [0], [0]

            def take_sums(b):
                if b < TBH * (len(GATHER) - 1):
                    act.wait_ge(sem["slots_used"], NSEL * (b + 1))
                else:
                    act.wait_ge(sem["loop_sums"], b - TBH * (len(GATHER) - 1) + 1)
                act.activation(htok[:, b // TBH % 2, b % TBH], acc[:].rearrange("p a b -> p (a b)"), ACT.Copy)\
                   .then_inc(sem["otok_ready"], 1)

            def catch_up(x):
                for at in range(here[0], min(x, window[1]) + 1):
                    here[0] = at
                    keep_step(at)

            def keep_step(x):
                while activated[0] < min(x + 1, window[1]):
                    s = activated[0]
                    activated[0] += 1
                    at = slice(PAIR * s % NSLOT, PAIR * s % NSLOT + PAIR)
                    act.wait_ge(sem["dot_ready"], PAIR * (s + 1))
                    act.activation(acts[:, at], dots[:, at], ACT.Gelu).then_inc(sem["gelu_ready"], 1)
                while summed[0] < x // BLOCK_STEPS:
                    take_sums(summed[0])
                    summed[0] += 1

            keep_up[act.engine] = catch_up
            open_window(None)

            def x_is_ready(key):
                kind, l, hf = key
                if kind == "gla":
                    act.wait_ge(sem["x_loaded"], 16)
                elif kind == "fox":
                    act.wait_ge(x_ffn[0][hf], DC * TBH)
                else:
                    catch_up(position[f"mix{l}{hf}.{DC - 1}"])
                    act.wait_ge(x_mix[l][hf], DC)

            def adaln(key):
                kind, l, hf = key
                n = LN[key]
                x_is_ready(key)
                if n:
                    prev = [k for k in LN if LN[k] == n - 1][0]
                    full(act, {"gla": f"v{prev[2]}.{DC - 1}", "route": f"pq{RT.get(prev[1:])}.{HP - 1}",
                               "fox": f"fg{prev[2]}.{DC - 1}"}[prev[0]])
                act.activation(hT[:], xT[:, :, half_of(hf)], ACT.Square).then_inc(sem["sq_ready"], 1)
                catch_up(position[f"ms{n}"])
                act.wait_ge(sem["ms_ready"], n + 1)
                act.activation(rms[:], rms[:], ACT.Sqrt).then_inc(sem["rms_ready"], 1)
                act.wait_ge(sem["mods_ready"], 3 if l == 1 else (1 if kind == "gla" else 2))
                if kind == "fox":
                    for c in range(DC):
                        act.wait_ge(sem["xn_ready"], 2 * n + 1 + 2 * c // DC)
                        act.activation(f_hk[:, c], hT[:, c], ACT.Identity, bias=mod[:, 96 + c:97 + c],
                                       scale=mod1[:, 104 + c:105 + c]).then_inc(sem["hk_ready"], 1)
                base = 48 * l + (24 if kind == "route" else 0)
                for c in range(DC):
                    act.wait_ge(sem["xn_ready"], 2 * n + 1 + 2 * c // DC)
                    act.activation(hT[:, c], hT[:, c], ACT.Identity, bias=mod[:, base + c:base + c + 1],
                                   scale=mod1[:, base + 8 + c:base + 9 + c]).then_inc(sem["h_ready"], 1)

            def take(name, dst, scale=1.0, src=None):
                full(act, name)
                b = bank_of(name)[:]
                freed(act.activation(dst, src(b) if src else b, ACT.Copy, scale=scale), name)

            def take_mods(name, rows, tiles):
                catch_up(position[name])
                act.wait_ge(sem["mod_tiles"], tiles)
                freed(act.activation(rows, bank_of(name)[0:MR, 0:rows.shape[1]], ACT.Copy), name)

            def left(b):
                return b[:, 0:HALF]

            def left2(b):
                return b[:, 0:HALF].rearrange("p (a b) -> p a b", a=TBH)

            def four(b):
                return b.rearrange("p (a b) -> p a b", a=4)

            def gla(key):
                g = key[2]
                adaln(key)
                take(f"glow{g}", g_low, src=lambda b: b[0:RANK, 0:HALF])
                take(f"q{g}.0", g_q[:, 0], GLA_HK ** -0.5, left)
                catch_up(position[f"gate{g}.1"])
                act.wait_ge(sem["gate_abs"], g + 1)
                link(act.activation(g_e, g_e, ACT.Exp))
                act.activation(g_e, g_e, ACT.Ln, bias=1.0).then_inc(sem["gate_soft"], 1)
                for h in range(1, GLA_H):
                    take(f"q{g}.{h}", g_q[:, h], GLA_HK ** -0.5, left)
                for h in range(GLA_H):
                    take(f"k{g}.{h}", g_k[:, h], 1.0, left)
                for lev in range(8):
                    if lev < 7:
                        act.wait_ge(sem["level_gap"], 7 * g + lev + 1)
                        act.activation(g_e, g_e, ACT.Exp, scale=1.0 / 16).then_inc(sem["level_exp"], 1)
                    for i in (2 * lev, 2 * lev + 1):
                        if i < DC:
                            take(f"g{g}.{i}", g_g[:, i], 1.0, left)
                        else:
                            c = i - DC
                            take(f"v{g}.{c}", g_v[:, :, c * P:(c + 1) * P], 1.0, left2)
                    if lev >= 4:
                        pair = 4 * g + lev - 4
                        taken(act, f"g{g}.{2 * (lev - 4) + 1}")
                        if pair:
                            act.wait_ge(sem["silu_done"], pair)
                        act.activation(g_sig, g_g[:, 2 * (lev - 4):2 * (lev - 4) + 2], ACT.Exp, scale=-1.0)\
                           .then_inc(sem["silu_exp"], 1)
                act.wait_ge(sem["last_gap"], g + 1)
                act.activation(g_e, g_e, ACT.Exp, scale=1.0 / 16).then_inc(sem["last_exp"], 1)
                act.activation(g_d, g_b, ACT.Exp, scale=1.0 / 16).then_inc(sem["chunk_exp"], 1)
                for tb in range(TBH):
                    take(f"kd{g}.{tb}", g_kd[:, tb], 1.0, four)
                for tb in range(TBH):
                    for half in range(2):
                        take(f"o{g}.{tb}.{half}", g_o[:, 4 * half:4 * half + 4, tb * P:(tb + 1) * P], 1.0, four)
                taken(act, f"o{g}.{TBH - 1}.1")
                act.wait_ge(sem["ql_ready"], 8 * (g + 1))
                act.wait_ge(sem["kl_ready"], 8 * (g + 1))
                act.activation(g_sq, g_o, ACT.Square).then_inc(sem["sqo_ready"], 1)
                catch_up(position[f"mso{g}.1"])
                act.wait_ge(sem["mso_ready"], g + 1)
                act.activation(g_rs, g_rs, ACT.Sqrt).then_inc(sem["rmso_ready"], 1)
                if g == 0:
                    take_mods("mod.1", mod_rows[1], 40)

            def route(key):
                r = RT[key[1:]]
                adaln(key)
                if r >= 2:
                    act.wait_ge(sem["dots_done"], r - 1)
                for b4 in range(4):
                    tb, half = b4 // 2, b4 % 2
                    take(f"htok{r}.{b4}", htok[:, r % 2, tb, half * 512:(half + 1) * 512])
                for j in range(HP):
                    take(f"pq{r}.{j}", r_q[:, j], 1.0, left)
                for tb in range(TBH):
                    n = TBH * r + tb
                    if tb:
                        catch_up(position["s_free", n])
                        act.wait_ge(sem["s_free"], n)
                        if n == 1:
                            open_block()
                    for b4 in range(4):
                        take(f"s{r}.{tb}.{b4}", r_s[:, 4 * b4:4 * b4 + 4], 1.0, four)
                    if n == 0:
                        take_mods("mod.2a", mod_rows[2][:, 0:128], 48)
                    catch_up(position["top_ready", n + 1])
                    act.wait_ge(sem["top_ready"], n + 1)
                    act.activation(r_ts, r_ts, ACT.Exp).then_inc(sem["top_exp"], 1)
                if r == 0:
                    take_mods("mod.2b", mod_rows[2][:, 128:640], 80)
                    take_mods("mod.2c", mod_rows[2][:, 640:1152], NMOD)

            def gather(q):
                for b in range(TBH * q, TBH * q + TBH):
                    with act.Fori(0, NSEL // NSLOT) as i:
                        for pr in range(NSLOT // PAIR):
                            at = slice(PAIR * pr, PAIR * pr + PAIR)
                            act.wait_ge(sem["dot_ready"], i * NSLOT + (b * NSEL + PAIR * pr + PAIR))
                            act.activation(acts[:, at], dots[:, at], ACT.Gelu).then_inc(sem["gelu_ready"], 1)
                    take_sums(b)

            def fox(key):
                hf = key[2]
                adaln(key)
                catch_up(position[f"f{hf}"])
                act.wait_ge(sem["fgate_abs"], hf + 1)
                link(act.activation(f_a, f_a, ACT.Exp))
                act.activation(f_a, f_a, ACT.Ln, bias=1.0).then_inc(sem["fgate_soft"], 1)

                def square(x, after):
                    taken(act, after)
                    act.activation(f_sq, x, ACT.Square).then_inc(sem["fsq_ready"], 1)

                def root(sq_no):
                    catch_up(position[f"fms{hf}.{'kkqq'[sq_no]}{sq_no % 2}.1"])
                    act.wait_ge(sem["fms_ready"], 4 * hf + sq_no + 1)
                    act.activation(f_rs, f_rs, ACT.Sqrt).then_inc(sem["frms_ready"], 1)

                for c in range(DC):
                    take(f"fk{hf}.{c}", f_k[:, c, half_of(hf)], 1.0, left)

                def values(cs):
                    for c in cs:
                        take(f"fv{hf}.{c}", f_v[:, TBH * hf:TBH * hf + TBH, c * P:(c + 1) * P], 1.0, left2)

                def queries(cs):
                    for c in cs:
                        take(f"fq{hf}.{c}", f_q[:, c], 1.0, left)

                def gates(cs):
                    for c in cs:
                        take(f"fg{hf}.{c}", f_g[:, c], 1.0, left)

                square(f_k[:, 0:4, half_of(hf)], f"fk{hf}.{DC - 1}")
                values(range(0, 6))
                root(0)
                square(f_k[:, 4:8, half_of(hf)], f"fk{hf}.{DC - 1}")
                values(range(6, 8))
                queries(range(0, 2))
                root(1)
                queries(range(2, 8))
                square(f_q[:, 0:4], f"fq{hf}.{DC - 1}")
                gates(range(0, 6))
                root(2)
                square(f_q[:, 4:8], f"fq{hf}.{DC - 1}")
                gates(range(6, 8))
                root(3)
                taken(act, f"fg{hf}.{DC - 1}")
                act.activation(f_g, f_g, ACT.Exp, scale=-1.0).then_inc(sem["fsig_exp"], 1)

                nu = TBH * FOX_H

                def probs(u):
                    keys = (TBH * hf + u // FOX_H + 1) * P
                    catch_up(position[f"sc{hf}.{u}"])
                    act.wait_ge(sem["negmax_ready"], nu * hf + u + 1)
                    if u >= 2:
                        full(act, f"pt{hf}.{u - 2}")
                    act.activation(f_p[:, u % 2, 0:keys], bank_of(f"sc{hf}.{u}")[:, 0:keys], ACT.Exp,
                                   bias=f_nm[:, u % 2:u % 2 + 1], accum_out=f_sum[:, u % 2:u % 2 + 1])\
                       .then_inc(sem["p_ready"], 1)

                probs(0)
                for u in range(nu):
                    keys = (TBH * hf + u // FOX_H + 1) * P
                    if u + 1 < nu:
                        probs(u + 1)
                    if u >= 2:
                        catch_up(position[f"pt{hf}.{u}"])
                        act.wait_ge(sem["mixed"], nu * hf + u - 1)
                    take(f"pt{hf}.{u}", f_pt[:, u % 2, 0:keys], 1.0, lambda b: b[:, 0:keys])

            take_mods("mod.0", mod_rows[0], 16)
            for q, stages in PLAN:
                open_window(q)
                if q is not None and not stages:
                    gather(q)
                for key in stages:
                    {"gla": gla, "route": route, "fox": fox}[key[0]](key)
                    if key[0] == "route":
                        catch_up(end_of_window(q))

        @block.gpsimd
        def _(pool):
            fetched = [0]

            def catch_up(x):
                while fetched[0] < min(x + 4, window[1]):
                    s = fetched[0]
                    fetched[0] += 1
                    b = s // BLOCK_STEPS
                    if s % BLOCK_STEPS == 0:
                        pool.wait_ge(sem["route_ready"], b + 1)
                    at = PAIR * s - b * NSEL + b % TBH * NSEL
                    r = PAIR * s % NSLOT
                    if PAIR * s >= NSLOT:
                        pool.wait_ge(sem["slots_used"], PAIR * s + PAIR - NSLOT)
                    for i in range(PAIR):
                        pool.indirect_dma_start(ring[:, r + i], None, uv,
                                                bass.IndirectOffsetOnAxis(ap=idx[:, b // TBH % 2, at + i:at + i + 1], axis=0))\
                            .then_inc(row_ready[r + i], 16)

            keep_up[pool.engine] = catch_up
            open_window(None)

            def gla(key):
                g = key[2]
                taken(pool, f"k{g}.3")
                e3 = g_e.rearrange("p (a b) -> p a b", a=GLA_H)
                for lev in range(8):
                    if lev:
                        i = 2 * lev - 1 if lev < 7 else 15
                        catch_up(position[f"g{g}.{i}" if i < DC else f"v{g}.{i - DC}"])
                    if lev < 7:
                        pool.wait_ge(sem["level_exp"], 7 * g + lev + 1)
                    else:
                        pool.wait_ge(sem["last_exp"], g + 1)
                    if lev:
                        full(pool, f"lev{g}.{lev - 1}.{TBH - 1}")
                    pool.tensor_tensor(g_kl, g_k, e3, ALU.mult).then_inc(sem["kl_ready"], 1)

            def gather(q):
                for tb in range(TBH):
                    b = TBH * q + tb
                    pool.wait_ge(sem["route_ready"], b + 1)
                    with pool.Fori(0, NSEL // NSLOT) as i:
                        for pr in range(NSLOT // PAIR):
                            r = PAIR * pr
                            pool.wait_ge(sem["slots_used"], i * NSLOT + (b * NSEL + r + PAIR - NSLOT))
                            pool.nop(nofuse=True)
                            pool.tensor_copy(idx_now[:, r:r + PAIR], idx[:, q % 2, bass.ds(i * NSLOT + (tb * NSEL + r), PAIR)])\
                                .then_inc(sem["idx_staged"], 1)
                            pool.wait_ge(sem["idx_staged"], i * (NSLOT // PAIR) + (tb * NSEL // PAIR + pr + 1))
                            pool.nop(nofuse=True)
                            for s in range(r, r + PAIR):
                                pool.indirect_dma_start(ring[:, s], None, uv,
                                                        bass.IndirectOffsetOnAxis(ap=idx_now[:, s:s + 1], axis=0))\
                                    .then_inc(row_ready[s], 16)

            for q, stages in PLAN:
                open_window(q)
                if q is not None and not stages:
                    gather(q)
                for key in stages:
                    if key[0] == "gla":
                        gla(key)
                    if key[0] == "route":
                        catch_up(end_of_window(q))


def layout(inputs):
    import numpy as np

    a = {k: np.asarray(v) for k, v in inputs.items()}

    def tiles(w):
        return w.reshape(DC, P, -1, P).transpose(2, 1, 0, 3)

    def small(w):
        return w.reshape(DC, P, -1).transpose(1, 0, 2)

    def column(v):
        return v.reshape(-1, P).T

    gla_in = a["gla_w_in"][0]
    kvf = a["fox_w_kvf"]
    wide = GLA_IN_WIDE
    keys = a["peer_sub_keys"].reshape(2, HP, NK, P)
    wt = np.empty((NTILES, P, DC, P), np.float32)
    for name, part in (("mod0", tiles(a["mod_w"][0])), ("mod1", tiles(a["mod_w"][1])), ("kvmod", tiles(a["kv_mod_w"])),
                       ("gla_in", tiles(gla_in[:, :wide])), ("gla_out", tiles(a["gla_w_out"][0])),
                       ("pq0", tiles(a["peer_w_q"][0])), ("pq1", tiles(a["peer_w_q"][1])),
                       ("keys0", keys[0].reshape(2, 8, NK, P).transpose(0, 3, 1, 2)),
                       ("keys1", keys[1].reshape(2, 8, NK, P).transpose(0, 3, 1, 2)),
                       ("fox_kv", tiles(kvf[:, :2 * D])), ("fox_qg", tiles(a["fox_w_qg"][0])),
                       ("fox_out", tiles(a["fox_w_out"][0]))):
        wt[TILES[name]:TILES[name] + len(part)] = part
    uv = np.empty((2 * EXPERTS, 2 * D), np.float32)
    uv[:, :D] = a["peer_u"].reshape(-1, D)
    uv[:, D:] = a["peer_v"].reshape(-1, D)
    col = np.zeros((P, NCOL), np.float32)
    col[:, COL_C:COL_C + DC] = column(a["c"][0])
    col[:, COL_MODB:COL_MODB + 96] = column(a["mod_b"].reshape(-1))
    col[:, COL_MODB + 96:COL_MODB + NMOD] = column(a["kv_mod_b"])
    col[:, COL_BG:COL_BG + GLA_H] = column(a["gla_b_gate"][0])
    col[:, COL_ON:COL_ON + 2] = column(a["gla_o_norm"][0])
    for half in range(2):
        col[half * FOX_HD:(half + 1) * FOX_HD, COL_KN] = a["fox_k_norm"]
        col[half * FOX_HD:(half + 1) * FOX_HD, COL_QN] = a["fox_q_norm"][0]
    col[:FOX_H, COL_BF] = a["fox_b_f"]
    wsmall = np.stack([small(gla_in[:, wide:]), small(kvf[:, 2 * D:])], axis=1).reshape(P, -1)
    const = np.zeros((P, NCONST), np.float32)
    at = np.arange(P)
    row, colm = at[:, None], at[None, :]
    const[:, K_ID:K_ID + P] = row == colm
    const[:, K_ONE:K_ONE + P] = 1
    const[:, K_BD:K_BD + P] = row // FOX_HD == colm // FOX_HD
    const[:, K_NEG:K_NEG + P] = np.where(colm > row, -1e30, 0)
    mask = np.empty((P, 8, P), np.float32)
    for lev, half in enumerate(LEVELS + [0]):
        m = row == colm if not half else ((row // (2 * half) == colm // (2 * half))
                                          & (row % (2 * half) < half) & (colm % (2 * half) >= half))
        mask[:, lev] = m
    const[:, K_IOTA:K_IOTA + TOPK] = np.arange(TOPK)
    return {"xt": a["x"][0].T, "wt": wt, "uv": uv, "cols": col, "consts": const, "masks": mask.reshape(P, -1), "small": wsmall,
            "wgate": a["gla_w_gate2"][0]}


GLA_IN_WIDE = 2 * GLA_H * GLA_HK + 2 * GLA_H * GLA_HV


def kernel(**inputs):
    import numpy as np
    import concourse.bacc as bacc
    from concourse.bass_utils import run_bass_kernel_spmd

    arrays = {n: np.ascontiguousarray(v) for n, v in layout(inputs).items()}
    nc = bacc.Bacc("TRN2", target_bir_lowering=False, num_devices=1)
    args = [nc.dram_tensor(f"in_{n}", a.shape, mybir.dt.from_np(a.dtype), kind="ExternalInput").ap()
            for n, a in arrays.items()]
    args.append(nc.dram_tensor("out_xt", (D, SEQ), F32, kind="ExternalOutput").ap())
    build(nc, *args)
    r = run_bass_kernel_spmd(nc, [{f"in_{n}": v for n, v in arrays.items()}], core_ids=[0])
    return np.ascontiguousarray(r.results[0]["out_xt"].T)[None]
```
